# Optimizing a Trainium2 kernel written in Bass

```python
import math
import jax, jax.numpy as jnp
from jax import lax
import numpy as np

D_MODEL = 1024
BATCH = 1
SEQ = 512
DEPTH = 2

MIX_WIDTH = D_MODEL
DIFF_HEADS = 4
DIFF_D = D_MODEL // 16
DIFF_DV = 2 * DIFF_D
GLA_HEADS = 4
GLA_DV = D_MODEL // 8
GLA_DK = GLA_DV // 2
GLA_GATE_RANK = 16
GLA_GATE_NORMALIZER = 16.0
GLA_CHUNK = 64
PEER_HEADS = 8
PEER_N_KEYS = 128
PEER_N_EXPERTS = PEER_N_KEYS * PEER_N_KEYS
PEER_D_KEY = 256
PEER_TOPK = 16
PEER_TOKEN_BLOCK = 128
ATTN_Q_BLOCK = 128
RMS_EPS = 1e-6

IN_SIZES = (
    DIFF_HEADS * 2 * DIFF_D,
    DIFF_HEADS * 2 * DIFF_D,
    DIFF_HEADS * DIFF_DV,
    GLA_HEADS * GLA_DK,
    GLA_HEADS * GLA_DK,
    GLA_HEADS * GLA_DV,
    GLA_HEADS * GLA_DV,
    GLA_GATE_RANK,
)
IN_COLS = sum(IN_SIZES)

kernel_name = "hymba_diffattn_gla_peer"

def _split_points():
    pts, acc = [], 0
    for s in IN_SIZES[:-1]:
        acc += s
        pts.append(acc)
    return pts

def rms_norm(x, w):
    xf = x.astype(jnp.float32)
    y = xf * lax.rsqrt(jnp.mean(xf * xf, axis=-1, keepdims=True) + RMS_EPS)
    return (y * w.astype(jnp.float32)).astype(x.dtype)

def diff_attention(q, k, v, q_norm_w, k_norm_w, lam, lam_init, out_norm_w):
    B, T = q.shape[0], q.shape[1]
    q = rms_norm(q, q_norm_w) * (DIFF_D ** -0.5)
    k = rms_norm(k, k_norm_w)
    nb = T // ATTN_Q_BLOCK
    qb = q.reshape(B, nb, ATTN_Q_BLOCK, DIFF_HEADS, 2, DIFF_D).transpose(1, 0, 2, 3, 4, 5)
    kpos = jnp.arange(T)

    def block(args):
        qi, i = args
        s = jnp.einsum('bqhmd,bkhmd->bhmqk', qi, k, preferred_element_type=jnp.float32)
        qpos = i * ATTN_Q_BLOCK + jnp.arange(ATTN_Q_BLOCK)
        mask = kpos[None, :] <= qpos[:, None]
        p = jax.nn.softmax(jnp.where(mask, s, -jnp.inf), axis=-1)
        a = p[:, :, 0] - lam * p[:, :, 1]
        return jnp.einsum('bhqk,bkhe->bqhe', a.astype(v.dtype), v)

    o = lax.map(block, (qb, jnp.arange(nb)))
    o = o.transpose(1, 0, 2, 3, 4).reshape(B, T, DIFF_HEADS, DIFF_DV)
    o = rms_norm(o, out_norm_w) * (1.0 - lam_init)
    return o.reshape(B, T, DIFF_HEADS * DIFF_DV)

def gla_chunked(q, k, v, g_log, out_gate, out_norm_w):
    B, T = q.shape[0], q.shape[1]
    C = GLA_CHUNK
    n = T // C
    out_dtype = v.dtype

    def chunks(a):
        return a.astype(jnp.float32).reshape(B, n, C, GLA_HEADS, a.shape[-1]).transpose(0, 3, 1, 2, 4)

    qc = chunks(q) * (GLA_DK ** -0.5)
    kc, vc, gc = chunks(k), chunks(v), chunks(g_log)
    b = jnp.cumsum(gc, axis=3)
    b_last = b[:, :, :, -1:, :]
    q_dec = qc * jnp.exp(b)
    k_inv = kc * jnp.exp(-b)
    k_dec = kc * jnp.exp(b_last - b)
    causal = jnp.tril(jnp.ones((C, C), dtype=bool))
    A = jnp.where(causal, jnp.einsum('bhnid,bhnjd->bhnij', q_dec, k_inv), 0.0)
    o_intra = jnp.einsum('bhnij,bhnje->bhnie', A, vc)
    U = jnp.einsum('bhncd,bhnce->nbhde', k_dec, vc)
    decay = jnp.exp(b_last[:, :, :, 0, :]).transpose(2, 0, 1, 3)

    def step(S, inp):
        dec, u = inp
        return dec[..., None] * S + u, S

    S0 = jnp.zeros((B, GLA_HEADS, GLA_DK, GLA_DV), jnp.float32)
    _, S_prev = lax.scan(step, S0, (decay, U))
    o_inter = jnp.einsum('bhncd,nbhde->bhnce', q_dec, S_prev)
    o = (o_intra + o_inter).transpose(0, 2, 3, 1, 4).reshape(B, T, GLA_HEADS, GLA_DV)
    o = rms_norm(o, out_norm_w) * jax.nn.silu(out_gate.astype(jnp.float32))
    return o.reshape(B, T, GLA_HEADS * GLA_DV).astype(out_dtype)

def peer(h, w_q, sub_keys, u_tab, v_tab):
    B, T, D = h.shape
    nt = (B * T) // PEER_TOKEN_BLOCK
    hb = h.reshape(nt, PEER_TOKEN_BLOCK, D)
    tb, kk = PEER_TOKEN_BLOCK, PEER_TOPK

    def block(xb):
        q = (xb @ w_q).reshape(tb, PEER_HEADS, 2, PEER_D_KEY // 2)
        s = jnp.einsum('thcd,hckd->thck', q, sub_keys, preferred_element_type=jnp.float32)
        top_s, top_i = lax.top_k(s, kk)
        cand = top_s[:, :, 0, :, None] + top_s[:, :, 1, None, :]
        cand_idx = top_i[:, :, 0, :, None] * PEER_N_KEYS + top_i[:, :, 1, None, :]
        best_s, best_pos = lax.top_k(cand.reshape(tb, PEER_HEADS, kk * kk), kk)
        expert = jnp.take_along_axis(cand_idx.reshape(tb, PEER_HEADS, kk * kk), best_pos, axis=-1)
        gate = jax.nn.softmax(best_s, axis=-1)
        u = u_tab[expert]
        act = jax.nn.gelu(jnp.einsum('td,thkd->thk', xb, u, preferred_element_type=jnp.float32),
                          approximate=False)
        w = (gate * act).astype(xb.dtype)
        return jnp.einsum('thk,thkd->td', w, v_tab[expert])

    return lax.map(block, hb).reshape(B, T, D)

def setup_inputs(seed: int = 0) -> dict:
    key = jax.random.key(seed)
    ks = jax.random.split(key, 20)

    def nrm(k, shape, scale):
        return jax.random.normal(k, shape, jnp.float32) * scale

    return {
        "x": nrm(ks[0], (BATCH, SEQ, D_MODEL), 1.0),
        "attn_norm_w": 1.0 + nrm(ks[1], (DEPTH, D_MODEL), 0.02),
        "w_in": nrm(ks[2], (DEPTH, D_MODEL, IN_COLS), D_MODEL ** -0.5),
        "diff_q_norm_w": 1.0 + nrm(ks[3], (DEPTH, DIFF_D), 0.02),
        "diff_k_norm_w": 1.0 + nrm(ks[4], (DEPTH, DIFF_D), 0.02),
        "lambda_q1": nrm(ks[5], (DEPTH, DIFF_D), 0.1),
        "lambda_k1": nrm(ks[6], (DEPTH, DIFF_D), 0.1),
        "lambda_q2": nrm(ks[7], (DEPTH, DIFF_D), 0.1),
        "lambda_k2": nrm(ks[8], (DEPTH, DIFF_D), 0.1),
        "diff_out_norm_w": 1.0 + nrm(ks[9], (DEPTH, DIFF_DV), 0.02),
        "gla_gate_w2": nrm(ks[10], (DEPTH, GLA_GATE_RANK, GLA_HEADS * GLA_DK), GLA_GATE_RANK ** -0.5),
        "gla_gate_b": nrm(ks[11], (DEPTH, GLA_HEADS * GLA_DK), 0.01),
        "gla_out_norm_w": 1.0 + nrm(ks[12], (DEPTH, GLA_DV), 0.02),
        "w_out": nrm(ks[13], (DEPTH, MIX_WIDTH, D_MODEL), MIX_WIDTH ** -0.5),
        "ffn_norm_w": 1.0 + nrm(ks[14], (DEPTH, D_MODEL), 0.02),
        "peer_w_q": nrm(ks[15], (DEPTH, D_MODEL, PEER_HEADS * PEER_D_KEY), D_MODEL ** -0.5),
        "peer_sub_keys": nrm(ks[16], (DEPTH, PEER_HEADS, 2, PEER_N_KEYS, PEER_D_KEY // 2),
                             (PEER_D_KEY // 2) ** -0.5),
        "peer_u": nrm(ks[17], (DEPTH, PEER_N_EXPERTS, D_MODEL), D_MODEL ** -0.5),
        "peer_v": nrm(ks[18], (DEPTH, PEER_N_EXPERTS, D_MODEL), PEER_HEADS ** -0.5),
    }

def reference(x, attn_norm_w, w_in, diff_q_norm_w, diff_k_norm_w, lambda_q1, lambda_k1,
              lambda_q2, lambda_k2, diff_out_norm_w, gla_gate_w2, gla_gate_b, gla_out_norm_w,
              w_out, ffn_norm_w, peer_w_q, peer_sub_keys, peer_u, peer_v):
    B, T, _ = x.shape
    split_pts = _split_points()
    for l in range(DEPTH):
        h = rms_norm(x, attn_norm_w[l])
        proj = h @ w_in[l]
        d_q, d_k, d_v, g_q, g_k, g_v, g_out, g_lr = jnp.split(proj, split_pts, axis=-1)

        lam_init = 0.8 - 0.6 * math.exp(-0.3 * l)
        lam = (jnp.exp(jnp.sum(lambda_q1[l].astype(jnp.float32) * lambda_k1[l].astype(jnp.float32)))
               - jnp.exp(jnp.sum(lambda_q2[l].astype(jnp.float32) * lambda_k2[l].astype(jnp.float32)))
               + lam_init)
        diff_o = diff_attention(
            d_q.reshape(B, T, DIFF_HEADS, 2, DIFF_D),
            d_k.reshape(B, T, DIFF_HEADS, 2, DIFF_D),
            d_v.reshape(B, T, DIFF_HEADS, DIFF_DV),
            diff_q_norm_w[l], diff_k_norm_w[l], lam, lam_init, diff_out_norm_w[l])

        g_log = jax.nn.log_sigmoid((g_lr @ gla_gate_w2[l] + gla_gate_b[l]).astype(jnp.float32)) \
            / GLA_GATE_NORMALIZER
        gla_o = gla_chunked(
            g_q.reshape(B, T, GLA_HEADS, GLA_DK),
            g_k.reshape(B, T, GLA_HEADS, GLA_DK),
            g_v.reshape(B, T, GLA_HEADS, GLA_DV),
            g_log.reshape(B, T, GLA_HEADS, GLA_DK),
            g_out.reshape(B, T, GLA_HEADS, GLA_DV),
            gla_out_norm_w[l])

        mix = jnp.concatenate([diff_o.astype(x.dtype), gla_o.astype(x.dtype)], axis=-1)
        x = x + mix @ w_out[l]

        h = rms_norm(x, ffn_norm_w[l])
        x = x + peer(h, peer_w_q[l], peer_sub_keys[l], peer_u[l], peer_v[l])
    return x


_drawn_inputs = setup_inputs


def setup_inputs(seed=0):
    import zlib

    import numpy as np

    out = dict(_drawn_inputs(seed))
    spreads = {}
    factors = {'gla_gate_b': 4.12}
    for name, (base, spread) in spreads.items():
        noise = np.random.default_rng([zlib.crc32(name.encode()), seed]).standard_normal(out[name].shape)
        drawn = base * np.exp(spread * noise) if base else spread * noise
        out[name] = __import__('jax').numpy.asarray(drawn.astype(out[name].dtype))
    for name, factor in factors.items():
        out[name] = (out[name] * factor).astype(out[name].dtype)
    return out
```

```python
import math
from contextlib import ExitStack

import concourse.bass as bass
from concourse import mybir

F32 = mybir.dt.float32
U32 = mybir.dt.uint32
BF16 = mybir.dt.bfloat16
ALU = mybir.AluOpType
ACT = mybir.ActivationFunctionType
AX_X = mybir.AxisListType.X

P = 128
EPS = 1e-6
GLA_CHUNK = 64
GATE_NORMALIZER = 16.0
TOPK = 16
HALF = 2
W_COLS = 512
U_RING = 6
V_RING = 5
W_RING = 2
DIAGS = 4
ACT_BANKS = 3
DVE_BANKS = 3
SUBS = 4
V_EVERY = 4
PARTS = 55
PARTS_ALONE = 40
LEAD = 9
LOWEST = -3.0e38
MASKED = -1.0e30


class Count:

    def __init__(self):
        self.n = {}

    def next(self, name):
        self.n[name] = self.n.get(name, 0) + 1
        return self.n[name]


def trunk(nc, x, attn_norm_w, w_in, q_norm_w, k_norm_w, lq1, lk1, lq2, lk2, diff_norm_w, gate_w2, gate_b,
          gla_norm_w, w_out, ffn_norm_w, w_q, keys_t, peer_u, peer_v, out):
    _, SEQ, D = x.shape
    LAYERS = w_in.shape[0]
    RANK, GK = gate_w2.shape[1:]
    HD = diff_norm_w.shape[1]
    DD = q_norm_w.shape[1]
    QH = D // 2
    HEADS = QH // HD
    GD = GK // HEADS
    PAIRS = HEADS // 2
    KC = D // P
    TILES = SEQ // P
    HALVES = TILES // HALF
    FRONTS = LAYERS * HALVES
    GROUPS = keys_t.shape[2]
    KEYS = keys_t.shape[3]
    PH = GROUPS // 2
    EXPERTS = peer_u.shape[1]
    PROJ = 6
    GPC = W_COLS // P
    CHUNKS = LAYERS * TILES * PH
    SLOTS = TOPK
    SUB = SLOTS // SUBS
    QJ = GROUPS // GPC
    HPC = GPC // 2
    V_DVE = SLOTS // V_EVERY
    V_PE = SLOTS - V_DVE
    HTOK = HALF * P
    SMALL_LOADS = 16 * LAYERS * 11

    u_rows = peer_u.rearrange("l e d -> (l e) d")
    v_rows = peer_v.rearrange("l e d -> (l e) d")
    LAM_INIT = [0.8 - 0.6 * math.exp(-0.3 * l) for l in range(LAYERS)]

    act_groups, at = {}, 0
    for name, n in (("hT", 2 * HALF), ("proj", PROJ * HALF), ("lr", 1), ("qkT", 2 * HALF),
                    ("aT", HEADS * HALF), ("gla", 3 * HALF), ("mixT", 2 * HALF), ("h2T", 2 * HALF),
                    ("route", (GPC // 2 + HALF) * GROUPS // GPC)):
        act_groups[name] = at
        at += n
    ACT_GROUPS = at

    dve_groups, at = {}, 0
    for name, n in (("attn", 5 * HEADS // 2 * HALF), ("gla", 6 * HALF), ("out", D // W_COLS * HALF)):
        dve_groups[name] = at
        at += n
    DVE_GROUPS = at

    QS = GPC // 2 + HALF

    def read(k, name, n):
        return k * DVE_GROUPS + dve_groups[name] + n

    def emptied(k, name, n):
        return k * ACT_GROUPS + act_groups[name] + n

    with ExitStack() as ctx:
        def sb(name, shape, dt=F32):
            return ctx.enter_context(nc.sbuf_tensor(name, shape, dt))

        def sem(name):
            return ctx.enter_context(nc.semaphore(name))

        u_ring = sb("u_ring", [P, U_RING, D])
        v_ring = sb("v_ring", [P, V_RING, D])
        w_ring = sb("w_ring", [P, W_RING, KC, W_COLS])
        xs = sb("xs", [P, TILES, D])
        h2 = sb("h2", [P, TILES, D])
        hT = sb("hT", [P, KC, HTOK])
        mix = sb("mix", [P, HALF, D])
        h1 = mix
        work = sb("work", [P, 5 * D])
        dqk = work[:, 0:2 * D].rearrange("p (i c) -> p i c", i=HALF)
        gla_in = work[:, 2 * D:5 * D].rearrange("p (i c) -> p i c", i=HALF)
        probs = work[:, 0:2 * D].rearrange("p (m c) -> p m c", m=4)
        kT = sb("kT", [P, HEADS, SEQ])
        qT = sb("qT", [P, HEADS, HTOK])
        v_nat = sb("v_nat", [P, TILES, QH])
        hT_flat = hT[:, :, :].rearrange("p c t -> p (c t)")
        aT = hT_flat.rearrange("p (h c) -> p h c", h=HEADS)
        keysT = sb("keysT", [P, GROUPS, KEYS])
        norm_w = sb("norm_w", [P, 2, D])
        qk_w = sb("qk_w", [P, LAYERS, 2, DD])
        head_w = sb("head_w", [P, LAYERS, 2, HD])
        w_lr = sb("w_lr", [P, LAYERS, KC, RANK])
        w_gate = sb("w_gate", [RANK + 1, LAYERS, GK])
        lrT = sb("lrT", [RANK + 1, HTOK])
        lam_in = h2[:, TILES - 1, 0:4 * LAYERS * DD].rearrange("p (a l d) -> p a l d", a=4, l=LAYERS)
        lam_sum = sb("lam_sum", [P, 2, LAYERS])
        neg_lam = sb("neg_lam", [P, LAYERS])
        ident = sb("ident", [P, P])
        causal = sb("causal", [P, SEQ])
        tri = sb("tri", [P, P])
        suffix = sb("suffix", [P, P])
        in_chunk = sb("in_chunk", [P, 2])
        chunk_is = sb("chunk_is", [P, 2])
        iota = sb("iota", [P, TOPK])
        eps_c = sb("eps_c", [P, 1])
        one_c = sb("one_c", [P, 1])
        a_intra = sb("a_intra", [P, HEADS, P])
        qd, ki, kd, z, g_log = (work[:, j * GK:(j + 1) * GK] for j in range(5))
        sil = work[:, 5 * GK:5 * GK + QH]
        qkiT = hT_flat[:, 0:4 * P].rearrange("p (a t) -> p a t", a=4)
        kdc = hT_flat[:, 4 * P:4 * P + 2 * GK].rearrange("p (c k) -> p c k", c=2)
        decay = sb("decay", [P, PAIRS, 2])
        state = sb("state", [P, 2, PAIRS, 2 * HD])
        square = sb("square", [P, D])
        dot_out = sb("dot_out", [P, D])
        sq = sb("sq", [P, 2 * 2 * HEADS * HALF])
        seed_ln = sb("seed_ln", [P, 2 * 2 * HEADS * HALF])
        seed = sb("seed", [P, 2 * 2 * HEADS * HALF])
        ms = sb("ms", [P, 2 * 2 * HEADS * HALF])
        rs = sb("rs", [P, 2 * 2 * HEADS * HALF])
        neg_max = sb("neg_max", [P, 4])
        row_sum = sb("row_sum", [P, 4])
        row_inv = sb("row_inv", [P, 4])
        qpT = work[:, 0:2 * GPC * HTOK].rearrange("p (b g c) -> p b g c", b=2, g=GPC)
        scores = mix[:, :, :].rearrange("p i (b g k) -> p i b g k", b=2, k=KEYS)
        free = [2 * GPC * HTOK]

        def scratch(n, dt=F32):
            free[0] += n
            ap = work[:, free[0] - n:free[0]]
            return ap if dt == F32 else ap.bitcast(dt)

        PICKS = HPC * TOPK
        top_s = scratch(GPC * TOPK).rearrange("p (g k) -> p g k", k=TOPK)
        top_i = scratch(GPC * TOPK, U32).rearrange("p (g k) -> p g k", k=TOPK)
        top_f = scratch(GPC * TOPK).rearrange("p (g k) -> p g k", k=TOPK)
        cand = scratch(PICKS * TOPK).rearrange("p (h k) -> p h k", h=HPC)
        best = scratch(PICKS).rearrange("p (h k) -> p h k", h=HPC)
        expo = scratch(PICKS).rearrange("p (h k) -> p h k", h=HPC)
        pos = scratch(PICKS, U32)
        pos_ij = scratch(2 * PICKS, U32).rearrange("p (a k) -> p a k", a=2)
        pos_f = scratch(2 * PICKS).rearrange("p (a k) -> p a k", a=2)
        sel = scratch(2 * PICKS).rearrange("p (a k) -> p a k", a=2)
        pick = scratch(PICKS * TOPK)
        gsum = sb("gsum", [P, HPC])
        gates = sb("gates", [P, TILES, PH, TOPK])
        experts = sb("experts", [P, TILES, PH * TOPK], U32)
        dots = sb("dots", [P, 2, SLOTS])
        acts = sb("acts", [P, 2, SLOTS])
        wts = sb("wts", [P, 2, SLOTS])
        diag = sb("diag", [P, DIAGS, P])

        peer_acc = ctx.enter_context(nc.psum_tensor("peer_acc", [P, D], F32))
        act_bank = [ctx.enter_context(nc.psum_tensor(f"act_bank{i}", [P, 512], F32)) for i in range(ACT_BANKS)]
        dve_bank = [ctx.enter_context(nc.psum_tensor(f"dve_bank{i}", [P, 512], F32)) for i in range(DVE_BANKS)]

        x_loaded = sem("x_loaded")
        small_loaded = sem("small_loaded")
        attn_w_loaded = sem("attn_w_loaded")
        ffn_w_loaded = sem("ffn_w_loaded")
        keys_loaded = sem("keys_loaded")
        w_loaded = [sem(f"w_loaded{i}") for i in range(W_RING)]
        u_landed = [sem(f"u_landed{i}") for i in range(U_RING)]
        v_landed = [sem(f"v_landed{i}") for i in range(V_RING)]
        stored = sem("stored")
        consts_ready = sem("consts_ready")
        pool_step = sem("pool_step")
        act_step = sem("act_step")
        dve_step = sem("dve_step")
        prep_ready = sem("prep_ready")
        lam_exp = sem("lam_exp")
        act_filled = sem("act_filled")
        act_emptied = sem("act_emptied")
        dve_filled = sem("dve_filled")
        dve_emptied = sem("dve_emptied")
        sums_ready = sem("sums_ready")
        seed_ready = sem("seed_ready")
        squares_ready = sem("squares_ready")
        h1_ready = sem("h1_ready")
        h2_ready = sem("h2_ready")
        qk_ready = sem("qk_ready")
        scores_ready = sem("scores_ready")
        exp_ready = sem("exp_ready")
        a_ready = sem("a_ready")
        soft_ready = sem("soft_ready")
        g_ready = sem("g_ready")
        gla_ready = sem("gla_ready")
        silu_ready = sem("silu_ready")
        mix_ready = sem("mix_ready")
        gate_arg = sem("gate_arg")
        gate_exp = sem("gate_exp")
        routed = sem("routed")
        u_used = sem("u_used")
        act_ready = sem("act_ready")
        wts_ready = sem("wts_ready")
        diag_ready = sem("diag_ready")
        v_used = sem("v_used")
        v_added = sem("v_added")
        peer_added = sem("peer_added")

        block = ctx.enter_context(nc.Block())

        def by_vector(s):
            return s % V_EVERY == V_EVERY - 1

        def v_count(c, s):
            mine = s // V_EVERY + 1
            return c * V_DVE + mine if by_vector(s) else c * V_PE + s + 1 - s // V_EVERY

        def interleave(front, slots_u, slots_v, begin):
            parts = (None for k in range(FRONTS) for _ in front(k))
            for _ in range(PARTS_ALONE):
                next(parts)
            for sub in range(SUBS):
                slots_u(0, sub)
            for half in range(FRONTS):
                left = PARTS + (LEAD if half == 0 else 0)
                for c in range(half * HALF * PH, (half + 1) * HALF * PH):
                    begin(c)
                    for sub in range(SUBS):
                        if left:
                            next(parts, None)
                            left -= 1
                        if c + 1 < CHUNKS:
                            slots_u(c + 1, sub)
                        slots_v(c, sub)

        @block.sync
        def _(sp):
            for t in range(TILES):
                sp.dma_start(xs[:, t, :], x[0, t * P:(t + 1) * P, :]).then_inc(x_loaded, 16)
            sp.dma_start(norm_w[:, 0, :], attn_norm_w[0].partition_broadcast(P)).then_inc(attn_w_loaded, 16)

            used = []

            def load_w(n, source):
                if n >= W_RING:
                    sp.wait_ge(*used[n - W_RING])
                sp.dma_start(w_ring[:, n % W_RING], source).then_inc(w_loaded[n % W_RING], 16)

            n = 0
            for k in range(FRONTS):
                l = k // HALVES
                w_in_v = w_in[l].rearrange("(c p) n -> p c n", p=P)
                w_out_v = w_out[l].rearrange("(c p) n -> p c n", p=P)
                w_q_v = w_q[l].rearrange("(c p) n -> p c n", p=P)
                sources = [w_in_v[:, :, j * W_COLS:(j + 1) * W_COLS] for j in range(PROJ)]
                sources += [w_out_v[:, :, j * W_COLS:(j + 1) * W_COLS] for j in range(D // W_COLS)]
                sources += [w_q_v[:, :, j * W_COLS:(j + 1) * W_COLS] for j in range(GROUPS // GPC)]
                used += [(act_filled, emptied(k, "proj", HALF * (j + 1))) for j in range(PROJ)]
                used += [(dve_filled, read(k, "out", HALF * (j + 1))) for j in range(D // W_COLS)]
                used += [(act_filled, emptied(k, "route", QS * j + GPC // 2)) for j in range(QJ)]
                for j, source in enumerate(sources):
                    load_w(n, source)
                    n += 1
                    if k % HALVES == HALVES - 1 and l + 1 < LAYERS and j == 2:
                        sp.wait_ge(h1_ready, HALF * (k + 1))
                        sp.dma_start(norm_w[:, 0, :], attn_norm_w[l + 1].partition_broadcast(P)).then_inc(attn_w_loaded, 16)
                    if k % HALVES == 0 and l > 0 and j == 2:
                        sp.wait_ge(h2_ready, HALF * k)
                        sp.dma_start(norm_w[:, 1, :], ffn_norm_w[l].partition_broadcast(P)).then_inc(ffn_w_loaded, 16)
                        sp.wait_ge(act_filled, ACT_GROUPS * k)
                        sp.dma_start(keysT[:], keys_t[l]).then_inc(keys_loaded, 16)
                    if k == 0 and j == 1:
                        small = 0
                        for ll in range(LAYERS):
                            loads = [
                                (qk_w[:, ll, 0, :], q_norm_w[ll].partition_broadcast(P)),
                                (qk_w[:, ll, 1, :], k_norm_w[ll].partition_broadcast(P)),
                                (head_w[:, ll, 0, :], diff_norm_w[ll].partition_broadcast(P)),
                                (head_w[:, ll, 1, :], gla_norm_w[ll].partition_broadcast(P)),
                                (w_lr[:, ll], w_in[ll, :, PROJ * W_COLS:].rearrange("(c p) n -> p c n", p=P)),
                                (w_gate[0:RANK, ll, :], gate_w2[ll]),
                                (w_gate[RANK:RANK + 1, ll, :], gate_b[ll:ll + 1, :]),
                            ]
                            loads += [(lam_in[:, a, ll, :], v[ll].partition_broadcast(P))
                                      for a, v in enumerate((lq1, lk1, lq2, lk2))]
                            for to, of in loads:
                                sp.dma_start(to, of).then_inc(small_loaded, 16)
                                small += 16
                        assert small == SMALL_LOADS
                        sp.dma_start(norm_w[:, 1, :], ffn_norm_w[0].partition_broadcast(P)).then_inc(ffn_w_loaded, 16)
                        sp.dma_start(keysT[:], keys_t[0]).then_inc(keys_loaded, 16)
            for t in range(TILES):
                sp.wait_ge(peer_added, (LAYERS - 1) * TILES + t + 1)
                sp.dma_start(out[0, t * P:(t + 1) * P, :], xs[:, t, :]).then_inc(stored, 16)
            sp.wait_ge(stored, 16 * TILES)

        @block.gpsimd
        def _(pool):
            count = Count()

            def link(ins):
                ins.then_inc(pool_step, 1)
                pool.wait_ge(pool_step, count.next("step"))

            def keep(ap, op, base, mult, pattern, fill):
                link(pool.affine_select(out=ap, in_=ap, compare_op=op, fill=fill, base=base,
                                        pattern=pattern, channel_multiplier=mult))

            link(pool.memset(ident[:], 0.0))
            keep(ident[:], ALU.not_equal, 0, 1, [[-1, P]], 1.0)
            link(pool.memset(eps_c[:], EPS))
            link(pool.memset(one_c[:], 1.0))
            link(pool.memset(lrT[:], 1.0))
            link(pool.memset(causal[:], 0.0))
            keep(causal[:, SEQ - P:], ALU.is_ge, 0, 1, [[-1, P]], MASKED)
            link(pool.memset(tri[:], 1.0 / GATE_NORMALIZER))
            keep(tri[:], ALU.is_ge, 0, -1, [[1, P]], 0.0)
            link(pool.memset(tri[0:GLA_CHUNK, GLA_CHUNK:P], 0.0))
            link(pool.memset(suffix[:], 1.0 / GATE_NORMALIZER))
            keep(suffix[:], ALU.is_gt, 0, 1, [[-1, P]], 0.0)
            link(pool.memset(suffix[GLA_CHUNK:P, 0:GLA_CHUNK], 0.0))
            link(pool.memset(in_chunk[:], 0.0))
            link(pool.memset(in_chunk[0:GLA_CHUNK, 0:1], 1.0 / GATE_NORMALIZER))
            link(pool.memset(in_chunk[GLA_CHUNK:P, 1:2], 1.0 / GATE_NORMALIZER))
            link(pool.memset(chunk_is[:], 0.0))
            link(pool.memset(chunk_is[0:GLA_CHUNK, 0:1], 1.0))
            link(pool.memset(chunk_is[GLA_CHUNK:P, 1:2], 1.0))
            link(pool.memset(a_intra[:], 0.0))
            link(pool.memset(state[:], 0.0))
            pool.iota(iota[:], [[1, TOPK]], base=0, channel_multiplier=0,
                      allow_small_or_imprecise_dtypes=True).then_inc(consts_ready, 1)

            def gather(table, ring, depth, landed, c, s):
                n = c * SLOTS + s
                tile, head = divmod(c, PH)
                e = head * TOPK + s
                pool.indirect_dma_start(
                    ring[:, n % depth, :], None, table,
                    bass.IndirectOffsetOnAxis(ap=experts[:, tile % TILES, e:e + 1], axis=0),
                ).then_inc(landed[n % depth], 16)

            for c in range(-1, CHUNKS):
                if c + 1 < CHUNKS and (c + 1) % HPC == 0:
                    k, part = divmod(c + 1, HALF * PH)
                    i, head = divmod(part, PH)
                    pool.wait_ge(routed, (k * QJ + head // HPC) * HALF + i + 1)
                for s in range(SLOTS):
                    if c + 1 < CHUNKS:
                        n = (c + 1) * SLOTS + s
                        if n >= U_RING:
                            pool.wait_ge(u_used, n - U_RING + 1)
                        gather(u_rows, u_ring, U_RING, u_landed, c + 1, s)
                    if c >= 0:
                        n = c * SLOTS + s
                        if n >= V_RING:
                            old_c, old_s = divmod(n - V_RING, SLOTS)
                            pool.wait_ge(v_added if by_vector(old_s) else v_used, v_count(old_c, old_s))
                        gather(v_rows, v_ring, V_RING, v_landed, c, s)

        @block.scalar
        def _(act):
            count = Count()

            def link(ins):
                ins.then_inc(act_step, 1)
                act.wait_ge(act_step, count.next("step"))

            def bank():
                n = count.next("bank")
                act.wait_ge(act_filled, n)
                return act_bank[(n - 1) % ACT_BANKS]

            def empty(to, cols=512, rows=P):
                b = bank()
                nc.scalar.activation(to, b[0:rows, 0:cols], ACT.Copy).then_inc(act_emptied, 1)

            def rsqrt_seed(n, width):
                link(nc.scalar.activation(seed_ln[:, 0:n], sq[:, 0:n], ACT.Ln, bias=eps_c[:], scale=1.0 / width))
                nc.scalar.activation(seed[:, 0:n], seed_ln[:, 0:n], ACT.Exp, scale=-0.5).then_inc(seed_ready, 1)

            def stats(t):
                link(nc.scalar.activation(square[:], xs[:, t, :], ACT.Square, accum_out=sq[:, 0:1]))
                rsqrt_seed(1, D)

            act.wait_ge(consts_ready, 1)

            def front(k):
                l, t0 = k // HALVES, (k % HALVES) * HALF
                if k:
                    act.wait_ge(routed, k * QJ * HALF)
                for i in range(HALF):
                    if l == 0:
                        act.wait_ge(x_loaded, 16 * TILES)
                    else:
                        act.wait_ge(peer_added, (l - 1) * TILES + t0 + i + 1)
                    if i:
                        act.wait_ge(h1_ready, k * HALF + i)
                    stats(t0 + i)
                    for g in range(2):
                        empty(hT[:, 4 * g:4 * g + 4, i * P:(i + 1) * P])
                    yield
                for j in range(PROJ):
                    for i in range(HALF):
                        if j < 2:
                            to = dqk[:, i, j * QH:(j + 1) * QH]
                        elif j == 2:
                            to = v_nat[:, t0 + i, :]
                        else:
                            to = gla_in[:, i, (j - 3) * W_COLS:(j - 2) * W_COLS]
                        empty(to)
                        if i < HALF - 1:
                            yield
                    if j == PROJ - 1:
                        empty(lrT[0:RANK, :], HTOK, RANK)
                    yield
                if k == 0:
                    act.wait_ge(prep_ready, 1)
                    nc.scalar.activation(lam_sum[:], lam_sum[:], ACT.Exp).then_inc(lam_exp, 1)
                for i in range(HALF):
                    if i:
                        act.wait_ge(sums_ready, count.next("sums") )
                    nc.scalar.activation(square[:], dqk[:, i, :], ACT.Square).then_inc(squares_ready, 1)
                act.wait_ge(sums_ready, count.next("sums"))
                rsqrt_seed(HALF * 4 * HEADS, DD)
                yield
                for i in range(HALF):
                    empty(qT[:, :, i * P:(i + 1) * P])
                    empty(kT[:, :, (t0 + i) * P:(t0 + i + 1) * P])
                yield
                for i in range(HALF):
                    keys = (t0 + i + 1) * P
                    for hg in range(HEADS // 2):
                        act.wait_ge(scores_ready, count.next("scores"))
                        for m in range(4):
                            ins = nc.scalar.activation(probs[:, m, 0:keys], probs[:, m, 0:keys], ACT.Exp,
                                                       bias=neg_max[:, m:m + 1], accum_out=row_sum[:, m:m + 1])
                        ins.then_inc(exp_ready, 1)
                        yield
                        for h in (2 * hg, 2 * hg + 1):
                            empty(aT[:, h, 0:keys], keys)
                        yield
                for i in range(HALF):
                    act.wait_ge(dve_emptied, read(k, "gla", 6 * i + 1))
                    link(nc.scalar.activation(g_log, g_log, ACT.Exp, scale=-1.0))
                    nc.scalar.activation(g_log, g_log, ACT.Ln, bias=one_c[:]).then_inc(soft_ready, 1)
                    yield
                    b = bank()
                    nc.scalar.activation(qd, b[:, 0:GK], ACT.Exp)
                    nc.scalar.activation(ki, b[:, 0:GK], ACT.Exp, scale=-1.0)
                    nc.scalar.activation(kd, b[:, GK:2 * GK], ACT.Exp).then_inc(act_emptied, 1)
                    b = bank()
                    nc.scalar.activation(decay[:].rearrange("p a c -> p (a c)"), b[:, 0:4],
                                         ACT.Exp).then_inc(act_emptied, 1)
                    nc.scalar.activation(sil, gla_in[:, i, 2 * W_COLS:3 * W_COLS], ACT.Exp,
                                         scale=-1.0).then_inc(silu_ready, 1)
                    empty(qkiT)
                    yield
                    act.wait_ge(dve_emptied, read(k, "gla", 6 * (i + 1)))
                    nc.scalar.activation(square[:], mix[:, i, :], ACT.Square).then_inc(squares_ready, 1)
                    act.wait_ge(sums_ready, count.next("sums"))
                    rsqrt_seed(2 * HEADS, HD)
                    yield
                for i in range(HALF):
                    for g in range(2):
                        empty(hT[:, 4 * g:4 * g + 4, i * P:(i + 1) * P])
                yield
                for j in range(D // W_COLS):
                    yield
                for i in range(HALF):
                    act.wait_ge(dve_emptied, read(k, "out", HALF * (D // W_COLS - 1) + i + 1))
                    if i:
                        act.wait_ge(h2_ready, k * HALF + i)
                    stats(t0 + i)
                    for g in range(2):
                        empty(hT[:, 4 * g:4 * g + 4, i * P:(i + 1) * P])
                    yield
                for j in range(QJ):
                    for g in range(GPC // 2):
                        empty(qpT[:, j % 2, 2 * g:2 * g + 2, :])
                        yield
                    if j >= 2:
                        act.wait_ge(routed, (k * QJ + j - 1) * HALF)
                    for i in range(HALF):
                        empty(scores[:, i, j % 2])
                    yield
                    for i in range(HALF):
                        act.wait_ge(gate_arg, (k * QJ + j) * HALF + i + 1)
                        nc.scalar.activation(expo, expo, ACT.Exp).then_inc(gate_exp, 1)
                        yield

            def begin(c):
                act.wait_ge(u_used, (c + 1) * SLOTS)
                nc.scalar.activation(acts[:, c % 2, :], dots[:, c % 2, :], ACT.Gelu).then_inc(act_ready, 1)

            def slots_v(c, sub):
                if sub == 0:
                    act.wait_ge(wts_ready, c + 1)
                for s in range(sub * SUB, (sub + 1) * SUB):
                    if by_vector(s):
                        continue
                    n = v_count(c, s) - 1
                    if n >= DIAGS:
                        act.wait_ge(v_used, n - DIAGS + 1)
                    nc.scalar.activation(diag[:, n % DIAGS, :], ident[:], ACT.Copy,
                                         scale=wts[:, c % 2, s:s + 1]).then_inc(diag_ready, 1)

            interleave(front, lambda c, sub: None, slots_v, begin)

        @block.vector
        def _(dve):
            count = Count()

            def link(ins):
                ins.then_inc(dve_step, 1)
                dve.wait_ge(dve_step, count.next("step"))

            def tell(ins, sem, name):
                ins.then_inc(sem, 1)
                dve.wait_ge(sem, count.next(name))

            def bank():
                n = count.next("bank")
                dve.wait_ge(dve_filled, n)
                return dve_bank[(n - 1) % DVE_BANKS]

            def release(ins):
                tell(ins, dve_emptied, "emptied")

            def rsqrt(n, width):
                dve.wait_ge(seed_ready, count.next("seed"))
                nc.vector.tensor_scalar(ms[:, 0:n], sq[:, 0:n], 1.0 / width, EPS, ALU.mult, ALU.add)
                link(nc.vector.tensor_tensor(rs[:, 0:n], seed[:, 0:n], seed[:, 0:n], ALU.mult))
                link(nc.vector.tensor_tensor(rs[:, 0:n], rs[:, 0:n], ms[:, 0:n], ALU.mult))
                link(nc.vector.tensor_scalar(rs[:, 0:n], rs[:, 0:n], -0.5, 1.5, ALU.mult, ALU.add))
                link(nc.vector.tensor_tensor(rs[:, 0:n], rs[:, 0:n], seed[:, 0:n], ALU.mult))

            def over(ap, n, w):
                return ap.unsqueeze(2).to_broadcast([P, n, w])

            def each(ap, n, w):
                return ap.unsqueeze(1).to_broadcast([P, n, w])

            def prepare():
                dve.wait_ge(small_loaded, SMALL_LOADS)
                for a in range(2):
                    link(nc.vector.tensor_tensor(lam_in[:, 2 * a], lam_in[:, 2 * a], lam_in[:, 2 * a + 1], ALU.mult))
                    ins = nc.vector.tensor_reduce(lam_sum[:, a, :], lam_in[:, 2 * a], op=ALU.add, axis=AX_X)
                    if a == 0:
                        link(ins)
                ins.then_inc(prep_ready, 1)
                for l in range(LAYERS):
                    link(nc.vector.tensor_scalar_mul(qk_w[:, l, 0, :], qk_w[:, l, 0, :], DD ** -0.5))
                    link(nc.vector.tensor_scalar_mul(head_w[:, l, 0, :], head_w[:, l, 0, :], 1.0 - LAM_INIT[l]))

            dve.wait_ge(consts_ready, 1)

            def top16(values, tops, index, n):
                for g in range(n):
                    ins = nc.vector.max(tops[:, g, 0:8], values[:, g, :])
                link(ins)
                for g in range(n):
                    nc.vector.max_index(index[:, g, 0:8], tops[:, g, 0:8], values[:, g, :])
                for g in range(n):
                    ins = nc.vector.match_replace(values[:, g, :], tops[:, g, 0:8], values[:, g, :], LOWEST)
                link(ins)
                for g in range(n):
                    ins = nc.vector.max(tops[:, g, 8:16], values[:, g, :])
                link(ins)
                for g in range(n):
                    ins = nc.vector.max_index(index[:, g, 8:16], tops[:, g, 8:16], values[:, g, :])
                link(ins)

            def front(k):
                l, t0 = k // HALVES, (k % HALVES) * HALF
                dve.wait_ge(attn_w_loaded, 16 * (l + 1))
                for i in range(HALF):
                    rsqrt(1, D)
                    tell(nc.vector.scalar_tensor_tensor(out=h1[:, i, :], in0=xs[:, t0 + i, :], scalar=rs[:, 0:1],
                                                        in1=norm_w[:, 0, :], op0=ALU.mult, op1=ALU.mult),
                         h1_ready, "h1")
                    yield
                if k % HALVES == 0 and l > 0:
                    link(nc.vector.memset(state[:, 0], 0.0))
                if k == 0:
                    prepare()
                for j in range(PROJ * HALF):
                    yield
                for i in range(HALF):
                    n = 4 * HEADS
                    dve.wait_ge(squares_ready, count.next("squares"))
                    tell(nc.vector.tensor_reduce(sq[:, i * n:(i + 1) * n], square[:].rearrange("p (g d) -> p g d", d=DD),
                                                 op=ALU.add, axis=AX_X), sums_ready, "sums")
                rsqrt(HALF * n, DD)
                yield
                for i in range(HALF):
                    v = dqk[:, i, :].rearrange("p (g d) -> p g d", d=DD)
                    link(nc.vector.tensor_tensor(v, v, over(rs[:, i * n:(i + 1) * n], n, DD), ALU.mult))
                    for j in range(2):
                        v = dqk[:, i, j * QH:(j + 1) * QH].rearrange("p (g d) -> p g d", d=DD)
                        ins = nc.vector.tensor_tensor(v, v, each(qk_w[:, l, j, :], 2 * HEADS, DD), ALU.mult)
                        if j == 0:
                            link(ins)
                        else:
                            tell(ins, qk_ready, "qk")
                yield
                if k == 0:
                    dve.wait_ge(lam_exp, 1)
                    link(nc.vector.tensor_tensor(neg_lam[:], lam_sum[:, 1, :], lam_sum[:, 0, :], ALU.subtract))
                    for ll in range(LAYERS):
                        link(nc.vector.tensor_scalar_add(neg_lam[:, ll:ll + 1], neg_lam[:, ll:ll + 1], -LAM_INIT[ll]))
                for i in range(HALF):
                    keys = (t0 + i + 1) * P
                    for hg in range(HEADS // 2):
                        dve.wait_ge(act_emptied, emptied(k, "qkT", 2 * HALF))
                        for m in range(4):
                            b = bank()
                            release(nc.vector.tensor_tensor(probs[:, m, 0:keys], b[:, 0:keys],
                                                            causal[:, SEQ - keys:], ALU.add))
                        tell(nc.vector.tensor_reduce(neg_max[:], probs[:, :, 0:keys], op=ALU.max, axis=AX_X,
                                                     negate=True), scores_ready, "scores")
                        yield
                        dve.wait_ge(exp_ready, count.next("exp"))
                        link(nc.vector.reciprocal(row_inv[:], row_sum[:]))
                        for h in range(2):
                            link(nc.vector.tensor_tensor(row_inv[:, 2 * h + 1:2 * h + 2], row_inv[:, 2 * h + 1:2 * h + 2],
                                                         neg_lam[:, l:l + 1], ALU.mult))
                            link(nc.vector.tensor_scalar(probs[:, 2 * h, 0:keys], probs[:, 2 * h, 0:keys],
                                                         row_inv[:, 2 * h:2 * h + 1], None, ALU.mult))
                            ins = nc.vector.scalar_tensor_tensor(
                                out=probs[:, 2 * h, 0:keys], in0=probs[:, 2 * h + 1, 0:keys],
                                scalar=row_inv[:, 2 * h + 1:2 * h + 2], in1=probs[:, 2 * h, 0:keys],
                                op0=ALU.mult, op1=ALU.add)
                            if h == 0:
                                link(ins)
                        tell(ins, a_ready, "a")
                        b = bank()
                        release(nc.vector.tensor_copy(mix[:, i, hg * 2 * HD:(hg + 1) * 2 * HD], b[:, 0:2 * HD]))
                        yield
                for i in range(HALF):
                    b = bank()
                    link(nc.vector.tensor_scalar(z, b[:, 0:GK], 0.0, None, ALU.min))
                    release(nc.vector.scalar_tensor_tensor(out=g_log, in0=z, scalar=-2.0, in1=b[:, 0:GK],
                                                           op0=ALU.mult, op1=ALU.add))
                    dve.wait_ge(soft_ready, count.next("soft"))
                    tell(nc.vector.tensor_tensor(g_log, z, g_log, ALU.subtract), g_ready, "g")
                    yield
                    dve.wait_ge(act_emptied, emptied(k, "gla", 3 * i + 2))
                    link(nc.vector.tensor_tensor(kd, kd, gla_in[:, i, GK:2 * GK], ALU.mult))
                    for c in range(2):
                        link(nc.vector.tensor_scalar(kdc[:, c, :], kd, chunk_is[:, c:c + 1], None, ALU.mult))
                    link(nc.vector.tensor_tensor(ki, ki, gla_in[:, i, GK:2 * GK], ALU.mult))
                    tell(nc.vector.scalar_tensor_tensor(out=qd, in0=gla_in[:, i, 0:GK], scalar=GD ** -0.5,
                                                        in1=qd, op0=ALU.mult, op1=ALU.mult), gla_ready, "gla")
                    yield
                    mask = tri[:].bitcast(U32).unsqueeze(1).to_broadcast([P, 2, P])
                    for b2 in range(2):
                        b = bank()
                        release(nc.vector.copy_predicated(
                            a_intra[:].rearrange("p (h b) i -> p b h i", b=2)[:, b2], mask,
                            b[:, 0:2 * P].rearrange("p (h i) -> p h i", h=2)))
                    for c in range(2):
                        b = bank()
                        for pair in range(PAIRS):
                            for s in range(2):
                                rows = slice(s * GD, (s + 1) * GD)
                                cols = slice(s * HD, (s + 1) * HD)
                                if c == 1 and pair == 0 and s == 0:
                                    dve.wait_ge(dve_filled, count.n["bank"] + 1)
                                ins = nc.vector.scalar_tensor_tensor(
                                    out=state[rows, (c + 1) % 2, pair, cols], in0=state[rows, c, pair, cols],
                                    scalar=decay[rows, pair, c:c + 1],
                                    in1=b[rows, pair * 2 * HD + s * HD:pair * 2 * HD + (s + 1) * HD],
                                    op0=ALU.mult, op1=ALU.add)
                        release(ins)
                    b = bank()
                    release(nc.vector.tensor_copy(mix[:, i, QH:D], b[:]))
                    dve.wait_ge(silu_ready, count.next("silu"))
                    link(nc.vector.tensor_scalar_add(sil, sil, 1.0))
                    link(nc.vector.reciprocal(sil, sil))
                    link(nc.vector.tensor_tensor(sil, sil, gla_in[:, i, 2 * W_COLS:3 * W_COLS], ALU.mult))
                    dve.wait_ge(squares_ready, count.next("squares"))
                    tell(nc.vector.tensor_reduce(sq[:, 0:2 * HEADS], square[:].rearrange("p (g d) -> p g d", d=HD),
                                                 op=ALU.add, axis=AX_X), sums_ready, "sums")
                    rsqrt(2 * HEADS, HD)
                    m = mix[:, i, :].rearrange("p (g d) -> p g d", d=HD)
                    link(nc.vector.tensor_tensor(m, m, over(rs[:, 0:2 * HEADS], 2 * HEADS, HD), ALU.mult))
                    m = mix[:, i, :].rearrange("p (a h d) -> p a h d", a=2, d=HD)
                    hw = head_w[:, l].unsqueeze(2).to_broadcast([P, 2, HEADS, HD])
                    link(nc.vector.tensor_tensor(m, m, hw, ALU.mult))
                    tell(nc.vector.tensor_tensor(mix[:, i, QH:D], mix[:, i, QH:D], sil, ALU.mult), mix_ready, "mix")
                    yield
                yield
                for j in range(D // W_COLS):
                    for i in range(HALF):
                        b = bank()
                        v = xs[:, t0 + i, j * W_COLS:(j + 1) * W_COLS]
                        release(nc.vector.tensor_tensor(v, v, b[:], ALU.add))
                    yield
                dve.wait_ge(ffn_w_loaded, 16 * (l + 1))
                for i in range(HALF):
                    rsqrt(1, D)
                    tell(nc.vector.scalar_tensor_tensor(out=h2[:, t0 + i, :], in0=xs[:, t0 + i, :], scalar=rs[:, 0:1],
                                                        in1=norm_w[:, 1, :], op0=ALU.mult, op1=ALU.mult),
                         h2_ready, "h2")
                    yield
                for j in range(QJ):
                    for g in range(GPC // 2 + 1):
                        yield
                    for i in range(HALF):
                        route(k, l, t0, i, j)
                        yield

            def route(k, l, t0, i, j):
                t, heads = t0 + i, slice(j * HPC, (j + 1) * HPC)
                dve.wait_ge(act_emptied, emptied(k, "route", QS * j + GPC // 2 + i + 1))
                top16(scores[:, i, j % 2], top_s, top_i, GPC)
                link(nc.vector.tensor_copy(top_f, top_i))
                tops = top_s.rearrange("p (h c) k -> p h c k", c=2)
                square_of = [P, HPC, TOPK, TOPK]
                link(nc.vector.tensor_tensor(cand.rearrange("p h (a b) -> p h a b", b=TOPK),
                                             tops[:, :, 0, :].unsqueeze(3).to_broadcast(square_of),
                                             tops[:, :, 1, :].unsqueeze(2).to_broadcast(square_of), ALU.add))
                top16(cand, best, pos.rearrange("p (h k) -> p h k", h=HPC), HPC)
                tell(nc.vector.tensor_tensor(expo, best, over(best[:, :, 0], HPC, TOPK), ALU.subtract),
                     gate_arg, "gate_arg")
                nc.vector.tensor_scalar(pos_ij[:, 0, :], pos, 4, None, ALU.logical_shift_right)
                link(nc.vector.tensor_scalar(pos_ij[:, 1, :], pos, TOPK - 1, None, ALU.bitwise_and))
                link(nc.vector.tensor_copy(pos_f, pos_ij))
                fs = top_f.rearrange("p (h c) k -> p h c k", c=2)
                flat = pick.rearrange("p (n a) -> p n a", a=TOPK)
                four = pick.rearrange("p (h n a) -> p h n a", h=HPC, a=TOPK)
                for c in range(2):
                    link(nc.vector.tensor_tensor(flat, over(pos_f[:, c, :], PICKS, TOPK),
                                                 each(iota[:], PICKS, TOPK), ALU.is_equal))
                    link(nc.vector.tensor_tensor(four, four, fs[:, :, c, :].unsqueeze(2).to_broadcast(square_of),
                                                 ALU.mult))
                    link(nc.vector.tensor_reduce(sel[:, c, :], flat, op=ALU.add, axis=AX_X))
                link(nc.vector.scalar_tensor_tensor(out=sel[:, 0, :], in0=sel[:, 0, :], scalar=float(KEYS),
                                                    in1=sel[:, 1, :], op0=ALU.mult, op1=ALU.add))
                link(nc.vector.tensor_scalar_add(experts[:, t, j * PICKS:(j + 1) * PICKS], sel[:, 0, :],
                                                 float(l * EXPERTS)))
                dve.wait_ge(gate_exp, (k * QJ + j) * HALF + i + 1)
                link(nc.vector.tensor_reduce(gsum[:], expo, op=ALU.add, axis=AX_X))
                link(nc.vector.reciprocal(gsum[:], gsum[:]))
                tell(nc.vector.tensor_tensor(gates[:, t, heads], expo, over(gsum[:], HPC, TOPK), ALU.mult),
                     routed, "routed")

            def add_tile(tile):
                dve.wait_ge(v_used, (tile + 1) * PH * V_PE)
                v = xs[:, tile % TILES, :]
                tell(nc.vector.tensor_tensor(v, v, peer_acc[:], ALU.add), peer_added, "peer_added")

            def begin(c):
                if c % PH == 0 and c > 0:
                    add_tile(c // PH - 1)
                tile, head = divmod(c, PH)
                dve.wait_ge(act_ready, c + 1)
                tell(nc.vector.tensor_tensor(wts[:, c % 2, :], acts[:, c % 2, :], gates[:, tile % TILES, head, :],
                                             ALU.mult), wts_ready, "wts")

            def slots_u(c, sub):
                tile = c // PH
                for s in range(sub * SUB, (sub + 1) * SUB):
                    n = c * SLOTS + s
                    dve.wait_ge(u_landed[n % U_RING], 16 * (n // U_RING + 1))
                    tell(nc.vector.scalar_tensor_tensor(
                        out=dot_out[:], in0=u_ring[:, n % U_RING, :], scalar=1.0, in1=h2[:, tile % TILES, :],
                        op0=ALU.mult, op1=ALU.mult, accum_out=dots[:, c % 2, s:s + 1]), u_used, "u_used")

            def slots_v(c, sub):
                tile = c // PH
                for s in range(sub * SUB, (sub + 1) * SUB):
                    if not by_vector(s):
                        continue
                    n = c * SLOTS + s
                    dve.wait_ge(v_landed[n % V_RING], 16 * (n // V_RING + 1))
                    v = xs[:, tile % TILES, :]
                    tell(nc.vector.scalar_tensor_tensor(out=v, in0=v_ring[:, n % V_RING, :],
                                                        scalar=wts[:, c % 2, s:s + 1], in1=v,
                                                        op0=ALU.mult, op1=ALU.add), v_added, "v_added")

            interleave(front, slots_u, slots_v, begin)
            add_tile(LAYERS * TILES - 1)

        @block.tensor
        def _(pe):
            count = Count()
            weights = [0]

            def fill_act():
                n = count.next("act")
                if n > ACT_BANKS:
                    pe.wait_ge(act_emptied, n - ACT_BANKS)
                return act_bank[(n - 1) % ACT_BANKS]

            def fill_dve():
                n = count.next("dve")
                if n > DVE_BANKS:
                    pe.wait_ge(dve_emptied, n - DVE_BANKS)
                return dve_bank[(n - 1) % DVE_BANKS]

            def all_emptied():
                pe.wait_ge(act_emptied, count.n["act"])

            def flip(blocks):
                b = fill_act()
                for j, block_ in enumerate(blocks):
                    ins = nc.tensor.transpose(b[:, j * P:(j + 1) * P], block_, ident[:])
                ins.then_inc(act_filled, 1)

            def next_weights():
                n = weights[0]
                weights[0] += 1
                pe.wait_ge(w_loaded[n % W_RING], 16 * (n // W_RING + 1))
                return w_ring[:, n % W_RING]

            pe.wait_ge(consts_ready, 1)

            def front(k):
                l, t0 = k // HALVES, (k % HALVES) * HALF
                for i in range(HALF):
                    pe.wait_ge(h1_ready, k * HALF + i + 1)
                    for g in range(2):
                        flip([h1[:, i, (4 * g + j) * P:(4 * g + j + 1) * P] for j in range(4)])
                    yield
                all_emptied()
                for j in range(PROJ):
                    w = next_weights()
                    for i in range(HALF):
                        b = fill_act()
                        for c in range(KC):
                            ins = nc.tensor.matmul(b[:], hT[:, c, i * P:(i + 1) * P], w[:, c, :],
                                                   start=(c == 0), stop=(c == KC - 1))
                        ins.then_inc(act_filled, 1)
                        if i < HALF - 1:
                            yield
                    if j == PROJ - 1:
                        pe.wait_ge(small_loaded, SMALL_LOADS)
                        b = fill_act()
                        for c in range(KC):
                            ins = nc.tensor.matmul(b[0:RANK, 0:HTOK], w_lr[:, l, c, :], hT[:, c, :],
                                                   start=(c == 0), stop=(c == KC - 1))
                        ins.then_inc(act_filled, 1)
                    yield
                yield
                for i in range(HALF):
                    pe.wait_ge(qk_ready, k * HALF + i + 1)
                    for j in range(2):
                        flip([dqk[:, i, j * QH + h * P:j * QH + (h + 1) * P] for h in range(HEADS)])
                yield
                all_emptied()
                for i in range(HALF):
                    t = t0 + i
                    keys = (t + 1) * P
                    for hg in range(HEADS // 2):
                        for h in (2 * hg, 2 * hg + 1):
                            for m in range(2):
                                rows = slice(m * DD, (m + 1) * DD)
                                b = fill_dve()
                                nc.tensor.matmul(b[:, 0:keys], qT[rows, h, i * P:(i + 1) * P], kT[rows, h, 0:keys],
                                                 start=True, stop=True).then_inc(dve_filled, 1)
                        yield
                        pe.wait_ge(a_ready, (k * HALF + i) * (HEADS // 2) + hg + 1)
                        for h in range(2):
                            flip([probs[:, 2 * h, j * P:(j + 1) * P] for j in range(t + 1)])
                        all_emptied()
                        b = fill_dve()
                        for h in range(2):
                            head = 2 * hg + h
                            for j in range(t + 1):
                                ins = nc.tensor.matmul(b[:, h * HD:(h + 1) * HD], aT[:, head, j * P:(j + 1) * P],
                                                       v_nat[:, j, head * HD:(head + 1) * HD],
                                                       start=(j == 0), stop=(j == t))
                        ins.then_inc(dve_filled, 1)
                        yield
                for i in range(HALF):
                    T = k * HALF + i
                    b = fill_dve()
                    nc.tensor.matmul(b[:, 0:GK], lrT[:, i * P:(i + 1) * P], w_gate[:, l, :],
                                     start=True, stop=True).then_inc(dve_filled, 1)
                    yield
                    pe.wait_ge(g_ready, T + 1)
                    b = fill_act()
                    nc.tensor.matmul(b[:, 0:GK], tri[:], g_log, start=True, stop=True)
                    nc.tensor.matmul(b[:, GK:2 * GK], suffix[:], g_log, start=True, stop=True).then_inc(act_filled, 1)
                    b = fill_act()
                    for pair in range(PAIRS):
                        ins = nc.tensor.matmul(b[:, 2 * pair:2 * pair + 2], g_log[:, pair * P:(pair + 1) * P], in_chunk[:],
                                               start=True, stop=True)
                    ins.then_inc(act_filled, 1)
                    pe.wait_ge(gla_ready, T + 1)
                    flip([qd[:, 0:P], qd[:, P:2 * P], ki[:, 0:P], ki[:, P:2 * P]])
                    yield
                    all_emptied()
                    for s in range(2):
                        rows = slice(s * GD, (s + 1) * GD)
                        b = fill_dve()
                        for pair in range(PAIRS):
                            ins = nc.tensor.matmul(b[:, pair * P:(pair + 1) * P], qkiT[rows, 2 + pair, :],
                                                   qkiT[rows, pair, :], start=True, stop=True)
                        ins.then_inc(dve_filled, 1)
                    for c in range(2):
                        b = fill_dve()
                        for pair in range(PAIRS):
                            ins = nc.tensor.matmul(b[:, pair * 2 * HD:(pair + 1) * 2 * HD], kdc[:, c, pair * P:(pair + 1) * P],
                                                   gla_in[:, i, W_COLS + pair * 2 * HD:W_COLS + (pair + 1) * 2 * HD],
                                                   start=True, stop=True)
                        ins.then_inc(dve_filled, 1)
                    pe.wait_ge(dve_emptied, read(k, "gla", 6 * i + 4))
                    b = fill_dve()
                    for h in range(HEADS):
                        nc.tensor.matmul(b[:, h * HD:(h + 1) * HD], a_intra[:, h, :],
                                         gla_in[:, i, W_COLS + h * HD:W_COLS + (h + 1) * HD],
                                         start=(h == 0), stop=False, skip_group_check=True)
                    for c in range(2):
                        toks = slice(c * GLA_CHUNK, (c + 1) * GLA_CHUNK)
                        for pair in range(PAIRS):
                            ins = nc.tensor.matmul(b[toks, pair * 2 * HD:(pair + 1) * 2 * HD], qkiT[:, pair, toks],
                                                   state[:, c, pair, :], start=False,
                                                   stop=(c == 1 and pair == PAIRS - 1), skip_group_check=True)
                    ins.then_inc(dve_filled, 1)
                    yield
                for i in range(HALF):
                    pe.wait_ge(mix_ready, k * HALF + i + 1)
                    for g in range(2):
                        flip([mix[:, i, (4 * g + j) * P:(4 * g + j + 1) * P] for j in range(4)])
                yield
                all_emptied()
                for j in range(D // W_COLS):
                    w = next_weights()
                    for i in range(HALF):
                        b = fill_dve()
                        for c in range(KC):
                            ins = nc.tensor.matmul(b[:], hT[:, c, i * P:(i + 1) * P], w[:, c, :],
                                                   start=(c == 0), stop=(c == KC - 1))
                        ins.then_inc(dve_filled, 1)
                    yield
                for i in range(HALF):
                    pe.wait_ge(h2_ready, k * HALF + i + 1)
                    for g in range(2):
                        flip([h2[:, t0 + i, (4 * g + j) * P:(4 * g + j + 1) * P] for j in range(4)])
                    yield
                all_emptied()
                pe.wait_ge(keys_loaded, 16 * (l + 1))
                for j in range(QJ):
                    w = next_weights()
                    for g in range(GPC // 2):
                        b = fill_act()
                        for s in range(2):
                            cols = slice((2 * g + s) * P, (2 * g + s + 1) * P)
                            for c in range(KC):
                                ins = nc.tensor.matmul(b[:, s * HTOK:(s + 1) * HTOK], w[:, c, cols], hT[:, c, :],
                                                       start=(c == 0), stop=(c == KC - 1))
                        ins.then_inc(act_filled, 1)
                        yield
                    all_emptied()
                    for i in range(HALF):
                        b = fill_act()
                        for g in range(GPC):
                            ins = nc.tensor.matmul(b[:, g * P:(g + 1) * P], qpT[:, j % 2, g, i * P:(i + 1) * P],
                                                   keysT[:, GPC * j + g, :], start=True, stop=True)
                        ins.then_inc(act_filled, 1)
                    yield
                    for i in range(HALF):
                        yield

            def slots_v(c, sub):
                tile, head = divmod(c, PH)
                for s in range(sub * SUB, (sub + 1) * SUB):
                    if by_vector(s):
                        continue
                    n = c * SLOTS + s
                    e = head * TOPK + s
                    last = head == PH - 1 and v_count(c, s) == (c + 1) * V_PE
                    if e == 0 and tile > 0:
                        pe.wait_ge(peer_added, tile)
                    pe.wait_ge(v_landed[n % V_RING], 16 * (n // V_RING + 1))
                    pe.wait_ge(diag_ready, v_count(c, s))
                    for j in range(D // 512):
                        ins = nc.tensor.matmul(peer_acc[:, j * 512:(j + 1) * 512], diag[:, (v_count(c, s) - 1) % DIAGS, :],
                                               v_ring[:, n % V_RING, j * 512:(j + 1) * 512],
                                               start=(e == 0), stop=last)
                    ins.then_inc(v_used, 1)

            interleave(front, lambda c, sub: None, slots_v, lambda c: None)


_NAMES = ["x", "attn_norm_w", "w_in", "diff_q_norm_w", "diff_k_norm_w", "lambda_q1", "lambda_k1", "lambda_q2",
          "lambda_k2", "diff_out_norm_w", "gla_gate_w2", "gla_gate_b", "gla_out_norm_w", "w_out", "ffn_norm_w",
          "peer_w_q", "peer_sub_keys", "peer_u", "peer_v"]


def kernel(**inputs):
    import numpy as _np
    import concourse.bacc as _bacc
    from concourse import mybir as _mybir
    from concourse.bass_utils import run_bass_kernel_spmd as _run

    nc = _bacc.Bacc("TRN2", target_bir_lowering=False, num_devices=1, dynamic_dma_scratch_size=8192)
    arrays, args = {}, []
    for name in _NAMES:
        a = _np.asarray(inputs[name])
        if name == "peer_sub_keys":
            layers, heads, books, keys, width = a.shape
            a = a.transpose(0, 4, 1, 2, 3).reshape(layers, width, heads * books, keys)
        a = _np.ascontiguousarray(a)
        arrays[f"in_{name}"] = a
        args.append(nc.dram_tensor(f"in_{name}", a.shape, _mybir.dt.from_np(a.dtype), kind="ExternalInput").ap())
    shape = tuple(inputs["x"].shape)
    args.append(nc.dram_tensor("out_0", shape, _mybir.dt.float32, kind="ExternalOutput").ap())
    trunk(nc, *args)
    r = _run(nc, [arrays], core_ids=[0])
    return r.results[0]["out_0"]
```

```python
import math
from contextlib import ExitStack

import concourse.bass as bass
from concourse import mybir

F32 = mybir.dt.float32
U32 = mybir.dt.uint32
BF16 = mybir.dt.bfloat16
ALU = mybir.AluOpType
ACT = mybir.ActivationFunctionType
AX_X = mybir.AxisListType.X

P = 128
EPS = 1e-6
GLA_CHUNK = 64
GATE_NORMALIZER = 16.0
TOPK = 16
HALF = 2
W_COLS = 512
U_RING = 6
V_RING = 6
W_RING = 2
DIAGS = 4
ACT_BANKS = 3
DVE_BANKS = 3
V_EVERY = 4
LEAD = 14
LOWEST = -3.0e38
MASKED = -1.0e30


class Count:

    def __init__(self):
        self.n = {}

    def next(self, name):
        self.n[name] = self.n.get(name, 0) + 1
        return self.n[name]


def trunk(nc, x, attn_norm_w, w_in, q_norm_w, k_norm_w, lq1, lk1, lq2, lk2, diff_norm_w, gate_w2, gate_b,
          gla_norm_w, w_out, ffn_norm_w, w_q, keys_t, peer_u, peer_v, out):
    _, SEQ, D = x.shape
    LAYERS = w_in.shape[0]
    RANK, GK = gate_w2.shape[1:]
    HD = diff_norm_w.shape[1]
    DD = q_norm_w.shape[1]
    QH = D // 2
    HEADS = QH // HD
    GD = GK // HEADS
    PAIRS = HEADS // 2
    KC = D // P
    TILES = SEQ // P
    HALVES = TILES // HALF
    FRONTS = LAYERS * HALVES
    GROUPS = keys_t.shape[2]
    KEYS = keys_t.shape[3]
    PH = GROUPS // 2
    EXPERTS = peer_u.shape[1]
    PROJ = 6
    GPC = W_COLS // P
    CHUNKS = LAYERS * TILES * PH
    SLOTS = TOPK
    QJ = GROUPS // GPC
    HPC = GPC // 2
    V_DVE = SLOTS // V_EVERY
    V_PE = SLOTS - V_DVE
    HTOK = HALF * P
    SMALL_LOADS = 16 * LAYERS * 11

    u_rows = peer_u.rearrange("l e d -> (l e) d")
    v_rows = peer_v.rearrange("l e d -> (l e) d")
    LAM_INIT = [0.8 - 0.6 * math.exp(-0.3 * l) for l in range(LAYERS)]

    NORM_PARTS = 5
    QK_PART = 4 * HALF
    PROJ_PARTS = 2 * PROJ * HALF + HALF + 2
    ATTN_STEP = 5
    ATTN_STEPS = HALF * HEADS // 2
    ATTN_PARTS = ATTN_STEPS * ATTN_STEP + 4
    GLA_STEP, GLA_TILE = 14, 19
    GLA_PARTS = (HALF - 1) * GLA_STEP + GLA_TILE + 2
    OUT_PARTS = 2 * HALF * D // W_COLS
    OUT_NORM_PARTS = OUT_PARTS + NORM_PARTS
    ROUTE_TILE = 5
    ROUTE_STEP = HALF * ROUTE_TILE
    ROUTE_LAG = 7
    ROUTE_PARTS = QJ * ROUTE_STEP + ROUTE_LAG
    PARTS = NORM_PARTS + PROJ_PARTS + ATTN_PARTS + GLA_PARTS + OUT_NORM_PARTS + ROUTE_PARTS
    PARTS_ALONE = PARTS - ROUTE_PARTS + ROUTE_LAG + ROUTE_TILE

    act_groups, at = {}, 0
    for name, n in (("hT", 2 * HALF), ("proj", PROJ * HALF), ("lr", 1), ("qkT", 2 * HALF),
                    ("aT", HEADS * HALF), ("gla", 3 * HALF), ("mixT", 2 * HALF), ("h2T", 2 * HALF),
                    ("route", (GPC // 2 + HALF) * GROUPS // GPC)):
        act_groups[name] = at
        at += n
    ACT_GROUPS = at

    dve_groups, at = {}, 0
    for name, n in (("attn", 5 * HEADS // 2 * HALF), ("gla", 6 * HALF), ("out", D // W_COLS * HALF)):
        dve_groups[name] = at
        at += n
    DVE_GROUPS = at

    QS = GPC // 2 + HALF

    def read(k, name, n):
        return k * DVE_GROUPS + dve_groups[name] + n

    def emptied(k, name, n):
        return k * ACT_GROUPS + act_groups[name] + n

    with ExitStack() as ctx:
        def sb(name, shape, dt=F32):
            return ctx.enter_context(nc.sbuf_tensor(name, shape, dt))

        def sem(name):
            return ctx.enter_context(nc.semaphore(name))

        u_ring = sb("u_ring", [P, U_RING, D])
        v_ring = sb("v_ring", [P, V_RING, D])
        w_ring = sb("w_ring", [P, W_RING, KC, W_COLS])
        xs = sb("xs", [P, TILES, D])
        h2 = sb("h2", [P, TILES, D])
        hT = sb("hT", [P, KC, HTOK])
        mix = sb("mix", [P, HALF, D])
        h1 = mix
        work = sb("work", [P, 5 * D])
        dqk = work[:, 0:2 * D].rearrange("p (i c) -> p i c", i=HALF)
        gla_in = work[:, 2 * D:5 * D].rearrange("p (i c) -> p i c", i=HALF)
        probs = work[:, 0:2 * D].rearrange("p (m c) -> p m c", m=4)
        kT = sb("kT", [P, HEADS, SEQ])
        qT = sb("qT", [P, HEADS, HTOK])
        v_nat = sb("v_nat", [P, TILES, QH])
        hT_flat = hT[:, :, :].rearrange("p c t -> p (c t)")
        aT = hT_flat.rearrange("p (h c) -> p h c", h=HEADS)
        keysT = sb("keysT", [P, GROUPS, KEYS])
        norm_w = sb("norm_w", [P, 2, D])
        qk_w = sb("qk_w", [P, LAYERS, 2, DD])
        head_w = sb("head_w", [P, LAYERS, 2, HD])
        w_lr = sb("w_lr", [P, LAYERS, KC, RANK])
        w_gate = sb("w_gate", [RANK + 1, LAYERS, GK])
        lrT = sb("lrT", [RANK + 1, HTOK])
        lam_in = h2[:, TILES - 1, 0:4 * LAYERS * DD].rearrange("p (a l d) -> p a l d", a=4, l=LAYERS)
        lam_sum = sb("lam_sum", [P, 2, LAYERS])
        neg_lam = sb("neg_lam", [P, LAYERS])
        ident = sb("ident", [P, P])
        causal = sb("causal", [P, SEQ])
        tri = sb("tri", [P, P])
        suffix = sb("suffix", [P, P])
        in_chunk = sb("in_chunk", [P, 2])
        chunk_is = sb("chunk_is", [P, 2])
        iota = sb("iota", [P, TOPK])
        eps_c = sb("eps_c", [P, 1])
        one_c = sb("one_c", [P, 1])
        a_intra = sb("a_intra", [P, HEADS, P])
        qd, ki, kd, z, g_log = (work[:, j * GK:(j + 1) * GK] for j in range(5))
        sil = work[:, 5 * GK:5 * GK + QH]
        qkiT = hT_flat[:, 0:4 * P].rearrange("p (a t) -> p a t", a=4)
        kdc = hT_flat[:, 4 * P:4 * P + 2 * GK].rearrange("p (c k) -> p c k", c=2)
        decay = sb("decay", [P, PAIRS, 2])
        state = sb("state", [P, 2, PAIRS, 2 * HD])
        square = sb("square", [P, D])
        sq = sb("sq", [P, 2 * 2 * HEADS * HALF])
        seed_ln = sb("seed_ln", [P, 2 * 2 * HEADS * HALF])
        seed = sb("seed", [P, 2 * 2 * HEADS * HALF])
        ms = sb("ms", [P, 2 * 2 * HEADS * HALF])
        rs = sb("rs", [P, 2 * 2 * HEADS * HALF])
        neg_max = sb("neg_max", [P, 4])
        row_sum = sb("row_sum", [P, 4])
        row_inv = sb("row_inv", [P, 4])
        qpT = work[:, 0:2 * GPC * HTOK].rearrange("p (b g c) -> p b g c", b=2, g=GPC)
        scores = mix[:, :, :].rearrange("p i (b g k) -> p i b g k", b=2, k=KEYS)
        free = [2 * GPC * HTOK]

        def scratch(n, dt=F32):
            free[0] += n
            ap = work[:, free[0] - n:free[0]]
            return ap if dt == F32 else ap.bitcast(dt)

        PICKS = HPC * TOPK
        top_s = scratch(GPC * TOPK).rearrange("p (g k) -> p g k", k=TOPK)
        top_i = scratch(GPC * TOPK, U32).rearrange("p (g k) -> p g k", k=TOPK)
        top_f = scratch(GPC * TOPK).rearrange("p (g k) -> p g k", k=TOPK)
        cand = scratch(PICKS * TOPK).rearrange("p (h k) -> p h k", h=HPC)
        best = scratch(PICKS).rearrange("p (h k) -> p h k", h=HPC)
        expo = scratch(PICKS).rearrange("p (h k) -> p h k", h=HPC)
        pos = scratch(PICKS, U32)
        pos_ij = scratch(2 * PICKS, U32).rearrange("p (a k) -> p a k", a=2)
        pos_f = scratch(2 * PICKS).rearrange("p (a k) -> p a k", a=2)
        sel = scratch(2 * PICKS).rearrange("p (a k) -> p a k", a=2)
        pick = scratch(PICKS * TOPK)
        gsum = sb("gsum", [P, HPC])
        gates = sb("gates", [P, TILES, PH, TOPK])
        experts = sb("experts", [P, TILES, PH * TOPK], U32)
        dots = sb("dots", [P, 2, SLOTS])
        acts = sb("acts", [P, 2, SLOTS])
        wts = sb("wts", [P, 2, SLOTS])
        diag = sb("diag", [P, DIAGS, P])

        peer_acc = ctx.enter_context(nc.psum_tensor("peer_acc", [P, D], F32))
        act_bank = [ctx.enter_context(nc.psum_tensor(f"act_bank{i}", [P, 512], F32)) for i in range(ACT_BANKS)]
        dve_bank = [ctx.enter_context(nc.psum_tensor(f"dve_bank{i}", [P, 512], F32)) for i in range(DVE_BANKS)]

        x_loaded = sem("x_loaded")
        small_loaded = sem("small_loaded")
        attn_w_loaded = sem("attn_w_loaded")
        ffn_w_loaded = sem("ffn_w_loaded")
        keys_loaded = sem("keys_loaded")
        w_loaded = [sem(f"w_loaded{i}") for i in range(W_RING)]
        u_landed = [sem(f"u_landed{i}") for i in range(U_RING)]
        v_landed = [sem(f"v_landed{i}") for i in range(V_RING)]
        stored = sem("stored")
        consts_ready = sem("consts_ready")
        pool_step = sem("pool_step")
        act_step = sem("act_step")
        dve_step = sem("dve_step")
        prep_ready = sem("prep_ready")
        lam_exp = sem("lam_exp")
        act_filled = sem("act_filled")
        act_emptied = sem("act_emptied")
        dve_filled = sem("dve_filled")
        dve_emptied = sem("dve_emptied")
        sums_ready = sem("sums_ready")
        seed_ready = sem("seed_ready")
        squares_ready = sem("squares_ready")
        h1_ready = sem("h1_ready")
        h2_ready = sem("h2_ready")
        qk_ready = sem("qk_ready")
        scores_ready = sem("scores_ready")
        exp_ready = sem("exp_ready")
        a_ready = sem("a_ready")
        soft_ready = sem("soft_ready")
        g_ready = sem("g_ready")
        gla_ready = sem("gla_ready")
        silu_ready = sem("silu_ready")
        mix_ready = sem("mix_ready")
        gate_arg = sem("gate_arg")
        gate_exp = sem("gate_exp")
        routed = sem("routed")
        u_used = sem("u_used")
        act_ready = sem("act_ready")
        wts_ready = sem("wts_ready")
        diag_ready = sem("diag_ready")
        v_used = sem("v_used")
        v_added = sem("v_added")
        peer_added = sem("peer_added")

        block = ctx.enter_context(nc.Block())

        def by_vector(s):
            return s % V_EVERY == V_EVERY - 1

        def v_count(c, s):
            mine = s // V_EVERY + 1
            return c * V_DVE + mine if by_vector(s) else c * V_PE + s + 1 - s // V_EVERY

        def interleave(front, slot_u, slot_v, begin):
            parts = (None for k in range(FRONTS) for _ in front(k))
            for _ in range(PARTS_ALONE):
                next(parts)
            for s in range(SLOTS):
                slot_u(0, s)
            done = 0
            for n in range(CHUNKS * SLOTS):
                c, s = divmod(n, SLOTS)
                if c + 1 < CHUNKS:
                    slot_u(c + 1, s)
                if s == 0:
                    begin(c)
                due = min(n + 1, LEAD) + (n + 1) * PARTS // (HALF * PH * SLOTS)
                for _ in range(due - done):
                    next(parts, None)
                done = due
                slot_v(c, s)

        @block.sync
        def _(sp):
            for t in range(TILES):
                sp.dma_start(xs[:, t, :], x[0, t * P:(t + 1) * P, :]).then_inc(x_loaded, 16)
            sp.dma_start(norm_w[:, 0, :], attn_norm_w[0].partition_broadcast(P)).then_inc(attn_w_loaded, 16)

            used = []

            def load_w(n, source):
                if n >= W_RING:
                    sp.wait_ge(*used[n - W_RING])
                sp.dma_start(w_ring[:, n % W_RING], source).then_inc(w_loaded[n % W_RING], 16)

            n = 0
            for k in range(FRONTS):
                l = k // HALVES
                w_in_v = w_in[l].rearrange("(c p) n -> p c n", p=P)
                w_out_v = w_out[l].rearrange("(c p) n -> p c n", p=P)
                w_q_v = w_q[l].rearrange("(c p) n -> p c n", p=P)
                sources = [w_in_v[:, :, j * W_COLS:(j + 1) * W_COLS] for j in range(PROJ)]
                sources += [w_out_v[:, :, j * W_COLS:(j + 1) * W_COLS] for j in range(D // W_COLS)]
                sources += [w_q_v[:, :, j * W_COLS:(j + 1) * W_COLS] for j in range(GROUPS // GPC)]
                used += [(act_filled, emptied(k, "proj", HALF * (j + 1))) for j in range(PROJ)]
                used += [(dve_filled, read(k, "out", HALF * (j + 1))) for j in range(D // W_COLS)]
                used += [(act_filled, emptied(k, "route", QS * j + GPC // 2)) for j in range(QJ)]
                for j, source in enumerate(sources):
                    load_w(n, source)
                    n += 1
                    if k % HALVES == HALVES - 1 and l + 1 < LAYERS and j == 2:
                        sp.wait_ge(h1_ready, HALF * (k + 1))
                        sp.dma_start(norm_w[:, 0, :], attn_norm_w[l + 1].partition_broadcast(P)).then_inc(attn_w_loaded, 16)
                    if k % HALVES == 0 and l > 0 and j == 2:
                        sp.wait_ge(h2_ready, HALF * k)
                        sp.dma_start(norm_w[:, 1, :], ffn_norm_w[l].partition_broadcast(P)).then_inc(ffn_w_loaded, 16)
                        sp.wait_ge(act_filled, ACT_GROUPS * k)
                        sp.dma_start(keysT[:], keys_t[l]).then_inc(keys_loaded, 16)
                    if k == 0 and j == 1:
                        small = 0
                        for ll in range(LAYERS):
                            loads = [
                                (qk_w[:, ll, 0, :], q_norm_w[ll].partition_broadcast(P)),
                                (qk_w[:, ll, 1, :], k_norm_w[ll].partition_broadcast(P)),
                                (head_w[:, ll, 0, :], diff_norm_w[ll].partition_broadcast(P)),
                                (head_w[:, ll, 1, :], gla_norm_w[ll].partition_broadcast(P)),
                                (w_lr[:, ll], w_in[ll, :, PROJ * W_COLS:].rearrange("(c p) n -> p c n", p=P)),
                                (w_gate[0:RANK, ll, :], gate_w2[ll]),
                                (w_gate[RANK:RANK + 1, ll, :], gate_b[ll:ll + 1, :]),
                            ]
                            loads += [(lam_in[:, a, ll, :], v[ll].partition_broadcast(P))
                                      for a, v in enumerate((lq1, lk1, lq2, lk2))]
                            for to, of in loads:
                                sp.dma_start(to, of).then_inc(small_loaded, 16)
                                small += 16
                        assert small == SMALL_LOADS
                        sp.dma_start(norm_w[:, 1, :], ffn_norm_w[0].partition_broadcast(P)).then_inc(ffn_w_loaded, 16)
                        sp.dma_start(keysT[:], keys_t[0]).then_inc(keys_loaded, 16)
            for t in range(TILES):
                sp.wait_ge(peer_added, (LAYERS - 1) * TILES + t + 1)
                sp.dma_start(out[0, t * P:(t + 1) * P, :], xs[:, t, :]).then_inc(stored, 16)
            sp.wait_ge(stored, 16 * TILES)

        @block.gpsimd
        def _(pool):
            count = Count()

            def link(ins):
                ins.then_inc(pool_step, 1)
                pool.wait_ge(pool_step, count.next("step"))

            def keep(ap, op, base, mult, pattern, fill):
                link(pool.affine_select(out=ap, in_=ap, compare_op=op, fill=fill, base=base,
                                        pattern=pattern, channel_multiplier=mult))

            link(pool.memset(ident[:], 0.0))
            keep(ident[:], ALU.not_equal, 0, 1, [[-1, P]], 1.0)
            link(pool.memset(eps_c[:], EPS))
            link(pool.memset(one_c[:], 1.0))
            link(pool.memset(lrT[:], 1.0))
            link(pool.memset(causal[:], 0.0))
            keep(causal[:, SEQ - P:], ALU.is_ge, 0, 1, [[-1, P]], MASKED)
            link(pool.memset(tri[:], 1.0 / GATE_NORMALIZER))
            keep(tri[:], ALU.is_ge, 0, -1, [[1, P]], 0.0)
            link(pool.memset(tri[0:GLA_CHUNK, GLA_CHUNK:P], 0.0))
            link(pool.memset(suffix[:], 1.0 / GATE_NORMALIZER))
            keep(suffix[:], ALU.is_gt, 0, 1, [[-1, P]], 0.0)
            link(pool.memset(suffix[GLA_CHUNK:P, 0:GLA_CHUNK], 0.0))
            link(pool.memset(in_chunk[:], 0.0))
            link(pool.memset(in_chunk[0:GLA_CHUNK, 0:1], 1.0 / GATE_NORMALIZER))
            link(pool.memset(in_chunk[GLA_CHUNK:P, 1:2], 1.0 / GATE_NORMALIZER))
            link(pool.memset(chunk_is[:], 0.0))
            link(pool.memset(chunk_is[0:GLA_CHUNK, 0:1], 1.0))
            link(pool.memset(chunk_is[GLA_CHUNK:P, 1:2], 1.0))
            link(pool.memset(a_intra[:], 0.0))
            link(pool.memset(state[:], 0.0))
            pool.iota(iota[:], [[1, TOPK]], base=0, channel_multiplier=0,
                      allow_small_or_imprecise_dtypes=True).then_inc(consts_ready, 1)

            def gather(table, ring, depth, landed, c, s):
                n = c * SLOTS + s
                tile, head = divmod(c, PH)
                e = head * TOPK + s
                pool.indirect_dma_start(
                    ring[:, n % depth, :], None, table,
                    bass.IndirectOffsetOnAxis(ap=experts[:, tile % TILES, e:e + 1], axis=0),
                ).then_inc(landed[n % depth], 16)

            for c in range(-1, CHUNKS):
                if c + 1 < CHUNKS and (c + 1) % HPC == 0:
                    k, part = divmod(c + 1, HALF * PH)
                    i, head = divmod(part, PH)
                    pool.wait_ge(routed, (k * QJ + head // HPC) * HALF + i + 1)
                for s in range(SLOTS):
                    if c + 1 < CHUNKS:
                        n = (c + 1) * SLOTS + s
                        if n >= U_RING:
                            pool.wait_ge(u_used, n - U_RING + 1)
                        gather(u_rows, u_ring, U_RING, u_landed, c + 1, s)
                    if c >= 0:
                        n = c * SLOTS + s
                        if n >= V_RING:
                            old_c, old_s = divmod(n - V_RING, SLOTS)
                            pool.wait_ge(v_added if by_vector(old_s) else v_used, v_count(old_c, old_s))
                        gather(v_rows, v_ring, V_RING, v_landed, c, s)

        @block.scalar
        def _(act):
            count = Count()

            def link(ins):
                ins.then_inc(act_step, 1)
                act.wait_ge(act_step, count.next("step"))

            def bank():
                n = count.next("bank")
                act.wait_ge(act_filled, n)
                return act_bank[(n - 1) % ACT_BANKS]

            def empty(to, cols=512, rows=P):
                b = bank()
                nc.scalar.activation(to, b[0:rows, 0:cols], ACT.Copy).then_inc(act_emptied, 1)

            def rsqrt_seed(cols, width):
                link(nc.scalar.activation(seed_ln[:, cols], sq[:, cols], ACT.Ln, bias=eps_c[:], scale=1.0 / width))
                nc.scalar.activation(seed[:, cols], seed_ln[:, cols], ACT.Exp, scale=-0.5).then_inc(seed_ready, 1)

            def stats(t, i):
                link(nc.scalar.activation(square[:], xs[:, t, :], ACT.Square, accum_out=sq[:, i:i + 1]))
                rsqrt_seed(slice(i, i + 1), D)

            def empty_hT(i):
                for g in range(2):
                    empty(hT[:, 4 * g:4 * g + 4, i * P:(i + 1) * P])

            act.wait_ge(consts_ready, 1)

            def front(k):
                l, t0 = k // HALVES, (k % HALVES) * HALF
                for p in range(NORM_PARTS):
                    if p < HALF:
                        if l == 0:
                            act.wait_ge(x_loaded, 16 * TILES)
                        else:
                            act.wait_ge(peer_added, (l - 1) * TILES + t0 + p + 1)
                        stats(t0 + p, p)
                    if p >= 3:
                        empty_hT(p - 3)
                    yield
                for p in range(PROJ_PARTS):
                    j, i = divmod(p // 2 - 1, HALF)
                    if p == 2 and k:
                        act.wait_ge(routed, k * QJ * HALF)
                    if p % 2 == 0 and 0 <= j < PROJ:
                        if j < 2:
                            empty(dqk[:, i, j * QH:(j + 1) * QH])
                        elif j == 2:
                            empty(v_nat[:, t0 + i, :])
                        else:
                            empty(gla_in[:, i, (j - 3) * W_COLS:(j - 2) * W_COLS])
                    if p == PROJ_PARTS - HALF - 1:
                        empty(lrT[0:RANK, :], HTOK, RANK)
                    if p >= PROJ_PARTS - HALF:
                        i = p - (PROJ_PARTS - HALF)
                        empty(qT[:, :, i * P:(i + 1) * P])
                        empty(kT[:, :, (t0 + i) * P:(t0 + i + 1) * P])
                    if p in (QK_PART + 1, QK_PART + 3):
                        i = (p - QK_PART) // 2
                        if i:
                            act.wait_ge(sums_ready, count.next("sums"))
                        act.wait_ge(act_emptied, emptied(k, "proj", 2 * HALF))
                        nc.scalar.activation(square[:], dqk[:, i, :], ACT.Square).then_inc(squares_ready, 1)
                    if p == QK_PART + 5:
                        act.wait_ge(sums_ready, count.next("sums"))
                        rsqrt_seed(slice(0, HALF * 4 * HEADS), DD)
                    if p == QK_PART + 6 and k == 0:
                        act.wait_ge(prep_ready, 1)
                        nc.scalar.activation(lam_sum[:], lam_sum[:], ACT.Exp).then_inc(lam_exp, 1)
                    yield
                for p in range(ATTN_PARTS):
                    step, part = divmod(p, ATTN_STEP)
                    if part == 1 and step > 0:
                        i, hg = divmod(step - 1, HEADS // 2)
                        keys = (t0 + i + 1) * P
                        for h in (2 * hg, 2 * hg + 1):
                            empty(aT[:, h, 0:keys], keys)
                    if part == 3 and step < ATTN_STEPS:
                        keys = (t0 + step // (HEADS // 2) + 1) * P
                        act.wait_ge(scores_ready, count.next("scores"))
                        for m in range(4):
                            ins = nc.scalar.activation(probs[:, m, 0:keys], probs[:, m, 0:keys], ACT.Exp,
                                                       bias=neg_max[:, m:m + 1], accum_out=row_sum[:, m:m + 1])
                        ins.then_inc(exp_ready, 1)
                    yield
                for p in range(GLA_PARTS):
                    for i in range(HALF):
                        linear(k, i, p - i * GLA_STEP)
                        if p == GLA_PARTS - 3 + 2 * i:
                            empty_hT(i)
                    yield
                for p in range(OUT_NORM_PARTS):
                    i, odd = divmod(p - (OUT_PARTS - 1), 2)
                    if 0 <= i < HALF and not odd:
                        act.wait_ge(dve_emptied, read(k, "out", HALF * (D // W_COLS - 1) + i + 1))
                        stats(t0 + i, i)
                    if p in (OUT_PARTS + 2, OUT_PARTS + 4):
                        empty_hT((p - OUT_PARTS - 2) // 2)
                    yield
                for p in range(ROUTE_PARTS):
                    j, part = divmod(p, ROUTE_STEP)
                    if j < QJ and part in (2, 4):
                        empty(qpT[:, j % 2, part - 2:part, :])
                    if j < QJ and part == 6:
                        if j >= 2:
                            act.wait_ge(routed, (k * QJ + j - 1) * HALF)
                        for i in range(HALF):
                            empty(scores[:, i, j % 2])
                    n, part = divmod(p - ROUTE_LAG, ROUTE_TILE)
                    if n >= 0 and part == 3:
                        act.wait_ge(gate_arg, k * QJ * HALF + n + 1)
                        nc.scalar.activation(expo, expo, ACT.Exp).then_inc(gate_exp, 1)
                    yield

            def linear(k, i, part):
                if part == 2:
                    act.wait_ge(dve_emptied, read(k, "gla", 6 * i + 1))
                    link(nc.scalar.activation(g_log, g_log, ACT.Exp, scale=-1.0))
                    nc.scalar.activation(g_log, g_log, ACT.Ln, bias=one_c[:]).then_inc(soft_ready, 1)
                if part == 5:
                    b = bank()
                    nc.scalar.activation(qd, b[:, 0:GK], ACT.Exp)
                    nc.scalar.activation(ki, b[:, 0:GK], ACT.Exp, scale=-1.0)
                    nc.scalar.activation(kd, b[:, GK:2 * GK], ACT.Exp).then_inc(act_emptied, 1)
                    b = bank()
                    nc.scalar.activation(decay[:].rearrange("p a c -> p (a c)"), b[:, 0:4],
                                         ACT.Exp).then_inc(act_emptied, 1)
                    if i:
                        act.wait_ge(mix_ready, k * HALF + i)
                    nc.scalar.activation(sil, gla_in[:, i, 2 * W_COLS:3 * W_COLS], ACT.Exp,
                                         scale=-1.0).then_inc(silu_ready, 1)
                if part == 8:
                    empty(qkiT)
                if part == 14:
                    act.wait_ge(dve_emptied, read(k, "gla", 6 * (i + 1)))
                    nc.scalar.activation(square[:], mix[:, i, :], ACT.Square).then_inc(squares_ready, 1)
                if part == 16:
                    act.wait_ge(sums_ready, count.next("sums"))
                    rsqrt_seed(slice(0, 2 * HEADS), HD)

            def begin(c):
                act.wait_ge(u_used, (c + 1) * SLOTS)
                nc.scalar.activation(acts[:, c % 2, :], dots[:, c % 2, :], ACT.Gelu).then_inc(act_ready, 1)

            def slot_v(c, s):
                if s == 0:
                    act.wait_ge(wts_ready, c + 1)
                if by_vector(s):
                    return
                n = v_count(c, s) - 1
                if n >= DIAGS:
                    act.wait_ge(v_used, n - DIAGS + 1)
                nc.scalar.activation(diag[:, n % DIAGS, :], ident[:], ACT.Copy,
                                     scale=wts[:, c % 2, s:s + 1]).then_inc(diag_ready, 1)

            interleave(front, lambda c, s: None, slot_v, begin)

        @block.vector
        def _(dve):
            count = Count()

            def link(ins):
                ins.then_inc(dve_step, 1)
                dve.wait_ge(dve_step, count.next("step"))

            def tell(ins, sem, name):
                ins.then_inc(sem, 1)
                dve.wait_ge(sem, count.next(name))

            def bank():
                n = count.next("bank")
                dve.wait_ge(dve_filled, n)
                return dve_bank[(n - 1) % DVE_BANKS]

            def release(ins):
                tell(ins, dve_emptied, "emptied")

            def rsqrt(cols, width):
                dve.wait_ge(seed_ready, count.next("seed"))
                nc.vector.tensor_scalar(ms[:, cols], sq[:, cols], 1.0 / width, EPS, ALU.mult, ALU.add)
                link(nc.vector.tensor_tensor(rs[:, cols], seed[:, cols], seed[:, cols], ALU.mult))
                link(nc.vector.tensor_tensor(rs[:, cols], rs[:, cols], ms[:, cols], ALU.mult))
                link(nc.vector.tensor_scalar(rs[:, cols], rs[:, cols], -0.5, 1.5, ALU.mult, ALU.add))
                link(nc.vector.tensor_tensor(rs[:, cols], rs[:, cols], seed[:, cols], ALU.mult))

            def norm(to, t, i, weight, ready, name):
                rsqrt(slice(i, i + 1), D)
                tell(nc.vector.scalar_tensor_tensor(out=to, in0=xs[:, t, :], scalar=rs[:, i:i + 1], in1=weight,
                                                    op0=ALU.mult, op1=ALU.mult), ready, name)

            def over(ap, n, w):
                return ap.unsqueeze(2).to_broadcast([P, n, w])

            def each(ap, n, w):
                return ap.unsqueeze(1).to_broadcast([P, n, w])

            def prepare():
                dve.wait_ge(small_loaded, SMALL_LOADS)
                for a in range(2):
                    link(nc.vector.tensor_tensor(lam_in[:, 2 * a], lam_in[:, 2 * a], lam_in[:, 2 * a + 1], ALU.mult))
                    ins = nc.vector.tensor_reduce(lam_sum[:, a, :], lam_in[:, 2 * a], op=ALU.add, axis=AX_X)
                    if a == 0:
                        link(ins)
                ins.then_inc(prep_ready, 1)
                for l in range(LAYERS):
                    link(nc.vector.tensor_scalar_mul(qk_w[:, l, 0, :], qk_w[:, l, 0, :], DD ** -0.5))
                    link(nc.vector.tensor_scalar_mul(head_w[:, l, 0, :], head_w[:, l, 0, :], 1.0 - LAM_INIT[l]))

            dve.wait_ge(consts_ready, 1)

            def first8(values, tops, index, n):
                for g in range(n):
                    ins = nc.vector.max(tops[:, g, 0:8], values[:, g, :])
                link(ins)
                for g in range(n):
                    nc.vector.max_index(index[:, g, 0:8], tops[:, g, 0:8], values[:, g, :])
                for g in range(n):
                    ins = nc.vector.match_replace(values[:, g, :], tops[:, g, 0:8], values[:, g, :], LOWEST)
                link(ins)

            def next8(values, tops, index, n):
                for g in range(n):
                    ins = nc.vector.max(tops[:, g, 8:16], values[:, g, :])
                link(ins)
                for g in range(n):
                    ins = nc.vector.max_index(index[:, g, 8:16], tops[:, g, 8:16], values[:, g, :])
                link(ins)

            def front(k):
                l, t0 = k // HALVES, (k % HALVES) * HALF
                n = 4 * HEADS
                dve.wait_ge(attn_w_loaded, 16 * (l + 1))
                for p in range(NORM_PARTS):
                    if 1 <= p <= HALF:
                        norm(h1[:, p - 1, :], t0 + p - 1, p - 1, norm_w[:, 0, :], h1_ready, "h1")
                    yield
                if k % HALVES == 0 and l > 0:
                    link(nc.vector.memset(state[:, 0], 0.0))
                if k == 0:
                    prepare()
                for p in range(PROJ_PARTS):
                    if p in (QK_PART + 2, QK_PART + 4):
                        i = (p - QK_PART) // 2 - 1
                        dve.wait_ge(squares_ready, count.next("squares"))
                        tell(nc.vector.tensor_reduce(sq[:, i * n:(i + 1) * n],
                                                     square[:].rearrange("p (g d) -> p g d", d=DD),
                                                     op=ALU.add, axis=AX_X), sums_ready, "sums")
                    if p == QK_PART + 6:
                        rsqrt(slice(0, HALF * n), DD)
                    if p in (QK_PART + 7, QK_PART + 8):
                        i = p - QK_PART - 7
                        v = dqk[:, i, :].rearrange("p (g d) -> p g d", d=DD)
                        link(nc.vector.tensor_tensor(v, v, over(rs[:, i * n:(i + 1) * n], n, DD), ALU.mult))
                        for j in range(2):
                            v = dqk[:, i, j * QH:(j + 1) * QH].rearrange("p (g d) -> p g d", d=DD)
                            ins = nc.vector.tensor_tensor(v, v, each(qk_w[:, l, j, :], 2 * HEADS, DD), ALU.mult)
                            if j == 0:
                                link(ins)
                            else:
                                tell(ins, qk_ready, "qk")
                    if p == QK_PART + 9 and k == 0:
                        dve.wait_ge(lam_exp, 1)
                        link(nc.vector.tensor_tensor(neg_lam[:], lam_sum[:, 1, :], lam_sum[:, 0, :], ALU.subtract))
                        for ll in range(LAYERS):
                            link(nc.vector.tensor_scalar_add(neg_lam[:, ll:ll + 1], neg_lam[:, ll:ll + 1],
                                                             -LAM_INIT[ll]))
                    yield
                for p in range(ATTN_PARTS):
                    step, part = divmod(p, ATTN_STEP)
                    keys = (t0 + step // (HEADS // 2) + 1) * P
                    if p == 1:
                        dve.wait_ge(act_emptied, emptied(k, "qkT", 2 * HALF))
                    if part in (1, 2) and step < ATTN_STEPS:
                        for m in (2 * part - 2, 2 * part - 1):
                            b = bank()
                            release(nc.vector.tensor_tensor(probs[:, m, 0:keys], b[:, 0:keys],
                                                            causal[:, SEQ - keys:], ALU.add))
                        if part == 2:
                            tell(nc.vector.tensor_reduce(neg_max[:], probs[:, :, 0:keys], op=ALU.max, axis=AX_X,
                                                         negate=True), scores_ready, "scores")
                    if part == 3 and step > 0:
                        i, hg = divmod(step - 1, HEADS // 2)
                        b = bank()
                        release(nc.vector.tensor_copy(mix[:, i, hg * 2 * HD:(hg + 1) * 2 * HD], b[:, 0:2 * HD]))
                    if part == 4:
                        dve.wait_ge(exp_ready, count.next("exp"))
                        link(nc.vector.reciprocal(row_inv[:], row_sum[:]))
                        for h in range(2):
                            link(nc.vector.tensor_tensor(row_inv[:, 2 * h + 1:2 * h + 2], row_inv[:, 2 * h + 1:2 * h + 2],
                                                         neg_lam[:, l:l + 1], ALU.mult))
                            link(nc.vector.tensor_scalar(probs[:, 2 * h, 0:keys], probs[:, 2 * h, 0:keys],
                                                         row_inv[:, 2 * h:2 * h + 1], None, ALU.mult))
                            ins = nc.vector.scalar_tensor_tensor(
                                out=probs[:, 2 * h, 0:keys], in0=probs[:, 2 * h + 1, 0:keys],
                                scalar=row_inv[:, 2 * h + 1:2 * h + 2], in1=probs[:, 2 * h, 0:keys],
                                op0=ALU.mult, op1=ALU.add)
                            if h == 0:
                                link(ins)
                        tell(ins, a_ready, "a")
                    yield
                for p in range(GLA_PARTS):
                    for i in range(HALF):
                        linear(l, i, p - i * GLA_STEP)
                    yield
                for p in range(OUT_NORM_PARTS):
                    group, odd = divmod(p - 2, 2)
                    if 0 <= group < OUT_PARTS // 2 and not odd:
                        j, i = divmod(group, HALF)
                        b = bank()
                        v = xs[:, t0 + i, j * W_COLS:(j + 1) * W_COLS]
                        release(nc.vector.tensor_tensor(v, v, b[:], ALU.add))
                    if p == 0:
                        dve.wait_ge(ffn_w_loaded, 16 * (l + 1))
                    if p in (OUT_PARTS, OUT_PARTS + 2):
                        i = (p - OUT_PARTS) // 2
                        norm(h2[:, t0 + i, :], t0 + i, i, norm_w[:, 1, :], h2_ready, "h2")
                    yield
                for p in range(ROUTE_PARTS):
                    n, part = divmod(p - ROUTE_LAG, ROUTE_TILE)
                    if n >= 0:
                        j, i = divmod(n, HALF)
                        route(k, l, t0, i, j, part)
                    yield

            def linear(l, i, part):
                if part == 1:
                    b = bank()
                    link(nc.vector.tensor_scalar(z, b[:, 0:GK], 0.0, None, ALU.min))
                    release(nc.vector.scalar_tensor_tensor(out=g_log, in0=z, scalar=-2.0, in1=b[:, 0:GK],
                                                           op0=ALU.mult, op1=ALU.add))
                if part == 3:
                    dve.wait_ge(soft_ready, count.next("soft"))
                    tell(nc.vector.tensor_tensor(g_log, z, g_log, ALU.subtract), g_ready, "g")
                if part == 6:
                    dve.wait_ge(silu_ready, count.next("silu"))
                    link(nc.vector.tensor_tensor(kd, kd, gla_in[:, i, GK:2 * GK], ALU.mult))
                    for c in range(2):
                        link(nc.vector.tensor_scalar(kdc[:, c, :], kd, chunk_is[:, c:c + 1], None, ALU.mult))
                    link(nc.vector.tensor_tensor(ki, ki, gla_in[:, i, GK:2 * GK], ALU.mult))
                    tell(nc.vector.scalar_tensor_tensor(out=qd, in0=gla_in[:, i, 0:GK], scalar=GD ** -0.5,
                                                        in1=qd, op0=ALU.mult, op1=ALU.mult), gla_ready, "gla")
                if part == 7:
                    link(nc.vector.tensor_scalar_add(sil, sil, 1.0))
                    link(nc.vector.reciprocal(sil, sil))
                if part == 8:
                    link(nc.vector.tensor_tensor(sil, sil, gla_in[:, i, 2 * W_COLS:3 * W_COLS], ALU.mult))
                if part == 10:
                    mask = tri[:].bitcast(U32).unsqueeze(1).to_broadcast([P, 2, P])
                    for b2 in range(2):
                        b = bank()
                        release(nc.vector.copy_predicated(
                            a_intra[:].rearrange("p (h b) i -> p b h i", b=2)[:, b2], mask,
                            b[:, 0:2 * P].rearrange("p (h i) -> p h i", h=2)))
                if part in (11, 13):
                    c = (part - 11) // 2
                    b = bank()
                    if c == 1:
                        dve.wait_ge(dve_filled, count.n["bank"] + 1)
                    for pair in range(PAIRS):
                        for s in range(2):
                            rows = slice(s * GD, (s + 1) * GD)
                            cols = slice(s * HD, (s + 1) * HD)
                            ins = nc.vector.scalar_tensor_tensor(
                                out=state[rows, (c + 1) % 2, pair, cols], in0=state[rows, c, pair, cols],
                                scalar=decay[rows, pair, c:c + 1],
                                in1=b[rows, pair * 2 * HD + s * HD:pair * 2 * HD + (s + 1) * HD],
                                op0=ALU.mult, op1=ALU.add)
                    release(ins)
                if part == 13:
                    b = bank()
                    release(nc.vector.tensor_copy(mix[:, i, QH:D], b[:]))
                if part == 15:
                    dve.wait_ge(squares_ready, count.next("squares"))
                    tell(nc.vector.tensor_reduce(sq[:, 0:2 * HEADS], square[:].rearrange("p (g d) -> p g d", d=HD),
                                                 op=ALU.add, axis=AX_X), sums_ready, "sums")
                if part == 17:
                    rsqrt(slice(0, 2 * HEADS), HD)
                    m = mix[:, i, :].rearrange("p (g d) -> p g d", d=HD)
                    link(nc.vector.tensor_tensor(m, m, over(rs[:, 0:2 * HEADS], 2 * HEADS, HD), ALU.mult))
                if part == 18:
                    m = mix[:, i, :].rearrange("p (a h d) -> p a h d", a=2, d=HD)
                    hw = head_w[:, l].unsqueeze(2).to_broadcast([P, 2, HEADS, HD])
                    link(nc.vector.tensor_tensor(m, m, hw, ALU.mult))
                    tell(nc.vector.tensor_tensor(mix[:, i, QH:D], mix[:, i, QH:D], sil, ALU.mult), mix_ready, "mix")

            def route(k, l, t0, i, j, part):
                t, heads = t0 + i, slice(j * HPC, (j + 1) * HPC)
                square_of = [P, HPC, TOPK, TOPK]
                best_pos = pos.rearrange("p (h k) -> p h k", h=HPC)
                fs = top_f.rearrange("p (h c) k -> p h c k", c=2)
                flat = pick.rearrange("p (n a) -> p n a", a=TOPK)
                four = pick.rearrange("p (h n a) -> p h n a", h=HPC, a=TOPK)

                def looked_up(c):
                    link(nc.vector.tensor_tensor(flat, over(pos_f[:, c, :], PICKS, TOPK),
                                                 each(iota[:], PICKS, TOPK), ALU.is_equal))
                    link(nc.vector.tensor_tensor(four, four, fs[:, :, c, :].unsqueeze(2).to_broadcast(square_of),
                                                 ALU.mult))
                    link(nc.vector.tensor_reduce(sel[:, c, :], flat, op=ALU.add, axis=AX_X))

                if part == 0:
                    dve.wait_ge(act_emptied, emptied(k, "route", QS * j + GPC // 2 + i + 1))
                    first8(scores[:, i, j % 2], top_s, top_i, GPC)
                if part == 1:
                    next8(scores[:, i, j % 2], top_s, top_i, GPC)
                    link(nc.vector.tensor_copy(top_f, top_i))
                    tops = top_s.rearrange("p (h c) k -> p h c k", c=2)
                    link(nc.vector.tensor_tensor(cand.rearrange("p h (a b) -> p h a b", b=TOPK),
                                                 tops[:, :, 0, :].unsqueeze(3).to_broadcast(square_of),
                                                 tops[:, :, 1, :].unsqueeze(2).to_broadcast(square_of), ALU.add))
                if part == 2:
                    first8(cand, best, best_pos, HPC)
                    next8(cand, best, best_pos, HPC)
                    tell(nc.vector.tensor_tensor(expo, best, over(best[:, :, 0], HPC, TOPK), ALU.subtract),
                         gate_arg, "gate_arg")
                if part == 3:
                    nc.vector.tensor_scalar(pos_ij[:, 0, :], pos, 4, None, ALU.logical_shift_right)
                    link(nc.vector.tensor_scalar(pos_ij[:, 1, :], pos, TOPK - 1, None, ALU.bitwise_and))
                    link(nc.vector.tensor_copy(pos_f, pos_ij))
                    looked_up(0)
                if part == 4:
                    looked_up(1)
                    dve.wait_ge(gate_exp, (k * QJ + j) * HALF + i + 1)
                    link(nc.vector.tensor_reduce(gsum[:], expo, op=ALU.add, axis=AX_X))
                    link(nc.vector.reciprocal(gsum[:], gsum[:]))
                    link(nc.vector.tensor_tensor(gates[:, t, heads], expo, over(gsum[:], HPC, TOPK), ALU.mult))
                    link(nc.vector.scalar_tensor_tensor(out=sel[:, 0, :], in0=sel[:, 0, :], scalar=float(KEYS),
                                                        in1=sel[:, 1, :], op0=ALU.mult, op1=ALU.add))
                    tell(nc.vector.tensor_scalar_add(experts[:, t, j * PICKS:(j + 1) * PICKS], sel[:, 0, :],
                                                     float(l * EXPERTS)), routed, "routed")

            def add_tile(tile):
                dve.wait_ge(v_used, (tile + 1) * PH * V_PE)
                v = xs[:, tile % TILES, :]
                tell(nc.vector.tensor_tensor(v, v, peer_acc[:], ALU.add), peer_added, "peer_added")

            def begin(c):
                if c % PH == 0 and c > 0:
                    add_tile(c // PH - 1)
                tile, head = divmod(c, PH)
                dve.wait_ge(act_ready, c + 1)
                tell(nc.vector.tensor_tensor(wts[:, c % 2, :], acts[:, c % 2, :], gates[:, tile % TILES, head, :],
                                             ALU.mult), wts_ready, "wts")

            def slot_u(c, s):
                tile, n = c // PH, c * SLOTS + s
                dve.wait_ge(u_landed[n % U_RING], 16 * (n // U_RING + 1))
                row = u_ring[:, n % U_RING, :]
                tell(nc.vector.scalar_tensor_tensor(
                    out=row, in0=row, scalar=1.0, in1=h2[:, tile % TILES, :],
                    op0=ALU.mult, op1=ALU.mult, accum_out=dots[:, c % 2, s:s + 1]), u_used, "u_used")

            def slot_v(c, s):
                if not by_vector(s):
                    return
                tile, n = c // PH, c * SLOTS + s
                dve.wait_ge(v_landed[n % V_RING], 16 * (n // V_RING + 1))
                v = xs[:, tile % TILES, :]
                tell(nc.vector.scalar_tensor_tensor(out=v, in0=v_ring[:, n % V_RING, :],
                                                    scalar=wts[:, c % 2, s:s + 1], in1=v,
                                                    op0=ALU.mult, op1=ALU.add), v_added, "v_added")

            interleave(front, slot_u, slot_v, begin)
            add_tile(LAYERS * TILES - 1)

        @block.tensor
        def _(pe):
            count = Count()
            weights = [0]

            def fill_act():
                n = count.next("act")
                if n > ACT_BANKS:
                    pe.wait_ge(act_emptied, n - ACT_BANKS)
                return act_bank[(n - 1) % ACT_BANKS]

            def fill_dve():
                n = count.next("dve")
                if n > DVE_BANKS:
                    pe.wait_ge(dve_emptied, n - DVE_BANKS)
                return dve_bank[(n - 1) % DVE_BANKS]

            def all_emptied():
                pe.wait_ge(act_emptied, count.n["act"])

            def flip(blocks):
                b = fill_act()
                for j, block_ in enumerate(blocks):
                    ins = nc.tensor.transpose(b[:, j * P:(j + 1) * P], block_, ident[:])
                ins.then_inc(act_filled, 1)

            def next_weights():
                n = weights[0]
                weights[0] += 1
                pe.wait_ge(w_loaded[n % W_RING], 16 * (n // W_RING + 1))
                return w_ring[:, n % W_RING]

            def flip_tile(source):
                for g in range(2):
                    flip([source[:, (4 * g + j) * P:(4 * g + j + 1) * P] for j in range(4)])

            def product(b, i, w, half):
                for c in range(half * KC // 2, (half + 1) * KC // 2):
                    ins = nc.tensor.matmul(b[:], hT[:, c, i * P:(i + 1) * P], w[:, c, :],
                                           start=(c == 0), stop=(c == KC - 1))
                return ins

            pe.wait_ge(consts_ready, 1)

            def front(k):
                l, t0 = k // HALVES, (k % HALVES) * HALF
                for p in range(NORM_PARTS):
                    if 2 <= p < 2 + HALF:
                        pe.wait_ge(h1_ready, k * HALF + p - 1)
                        flip_tile(h1[:, p - 2, :])
                    yield
                all_emptied()
                for p in range(PROJ_PARTS):
                    (j, i), half = divmod(p // 2, HALF), p % 2
                    if j < PROJ:
                        if half == 0:
                            if i == 0:
                                w = next_weights()
                            b = fill_act()
                        ins = product(b, i, w, half)
                        if half == 1:
                            ins.then_inc(act_filled, 1)
                    if p == PROJ_PARTS - HALF - 2:
                        pe.wait_ge(small_loaded, SMALL_LOADS)
                        b = fill_act()
                        for c in range(KC):
                            ins = nc.tensor.matmul(b[0:RANK, 0:HTOK], w_lr[:, l, c, :], hT[:, c, :],
                                                   start=(c == 0), stop=(c == KC - 1))
                        ins.then_inc(act_filled, 1)
                    i = p - (PROJ_PARTS - HALF - 1)
                    if 0 <= i < HALF:
                        pe.wait_ge(qk_ready, k * HALF + i + 1)
                        for j in range(2):
                            flip([dqk[:, i, j * QH + h * P:j * QH + (h + 1) * P] for h in range(HEADS)])
                    yield
                all_emptied()
                for p in range(ATTN_PARTS):
                    step, part = divmod(p, ATTN_STEP)
                    last_i, last_hg = divmod(step - 1, HEADS // 2)
                    last_tile = t0 + last_i
                    if part == 0 and step > 0:
                        pe.wait_ge(a_ready, k * ATTN_STEPS + step)
                        for h in range(2):
                            flip([probs[:, 2 * h, j * P:(j + 1) * P] for j in range(last_tile + 1)])
                    if part < 2 and step < ATTN_STEPS:
                        i, hg = divmod(step, HEADS // 2)
                        keys = (t0 + i + 1) * P
                        h = 2 * hg + part
                        for m in range(2):
                            rows = slice(m * DD, (m + 1) * DD)
                            b = fill_dve()
                            nc.tensor.matmul(b[:, 0:keys], qT[rows, h, i * P:(i + 1) * P], kT[rows, h, 0:keys],
                                             start=True, stop=True).then_inc(dve_filled, 1)
                    if part == 2 and step > 0:
                        all_emptied()
                        b = fill_dve()
                        for h in range(2):
                            head = 2 * last_hg + h
                            for j in range(last_tile + 1):
                                ins = nc.tensor.matmul(b[:, h * HD:(h + 1) * HD], aT[:, head, j * P:(j + 1) * P],
                                                       v_nat[:, j, head * HD:(head + 1) * HD],
                                                       start=(j == 0), stop=(j == last_tile))
                        ins.then_inc(dve_filled, 1)
                    yield
                for p in range(GLA_PARTS):
                    for i in range(HALF):
                        linear(k, l, i, p - i * GLA_STEP)
                        if p == GLA_PARTS - 4 + 2 * i:
                            pe.wait_ge(mix_ready, k * HALF + i + 1)
                            flip_tile(mix[:, i, :])
                    yield
                all_emptied()
                for p in range(OUT_NORM_PARTS):
                    (j, i), half = divmod(p // 2, HALF), p % 2
                    if p < OUT_PARTS:
                        if half == 0:
                            if i == 0:
                                w = next_weights()
                            b = fill_dve()
                        ins = product(b, i, w, half)
                        if half == 1:
                            ins.then_inc(dve_filled, 1)
                    if p in (OUT_PARTS + 1, OUT_PARTS + 3):
                        i = (p - OUT_PARTS) // 2
                        pe.wait_ge(h2_ready, k * HALF + i + 1)
                        flip_tile(h2[:, t0 + i, :])
                    yield
                all_emptied()
                pe.wait_ge(keys_loaded, 16 * (l + 1))
                for p in range(ROUTE_PARTS):
                    j, part = divmod(p, ROUTE_STEP)
                    if j < QJ and part < GPC:
                        if part == 0:
                            w = next_weights()
                        g, s = divmod(part, 2)
                        if s == 0:
                            b = fill_act()
                        for c in range(KC):
                            ins = nc.tensor.matmul(b[:, s * HTOK:(s + 1) * HTOK], w[:, c, part * P:(part + 1) * P],
                                                   hT[:, c, :], start=(c == 0), stop=(c == KC - 1))
                        if s == 1:
                            ins.then_inc(act_filled, 1)
                    if j < QJ and part == GPC + 1:
                        all_emptied()
                        for i in range(HALF):
                            b = fill_act()
                            for g in range(GPC):
                                ins = nc.tensor.matmul(b[:, g * P:(g + 1) * P], qpT[:, j % 2, g, i * P:(i + 1) * P],
                                                       keysT[:, GPC * j + g, :], start=True, stop=True)
                            ins.then_inc(act_filled, 1)
                    yield

            def linear(k, l, i, part):
                T = k * HALF + i
                if part == 0:
                    b = fill_dve()
                    nc.tensor.matmul(b[:, 0:GK], lrT[:, i * P:(i + 1) * P], w_gate[:, l, :],
                                     start=True, stop=True).then_inc(dve_filled, 1)
                if part == 4:
                    pe.wait_ge(g_ready, T + 1)
                    b = fill_act()
                    nc.tensor.matmul(b[:, 0:GK], tri[:], g_log, start=True, stop=True)
                    nc.tensor.matmul(b[:, GK:2 * GK], suffix[:], g_log, start=True, stop=True).then_inc(act_filled, 1)
                    b = fill_act()
                    for pair in range(PAIRS):
                        ins = nc.tensor.matmul(b[:, 2 * pair:2 * pair + 2], g_log[:, pair * P:(pair + 1) * P], in_chunk[:],
                                               start=True, stop=True)
                    ins.then_inc(act_filled, 1)
                if part == 7:
                    pe.wait_ge(gla_ready, T + 1)
                    flip([qd[:, 0:P], qd[:, P:2 * P], ki[:, 0:P], ki[:, P:2 * P]])
                if part == 9:
                    all_emptied()
                    for s in range(2):
                        rows = slice(s * GD, (s + 1) * GD)
                        b = fill_dve()
                        for pair in range(PAIRS):
                            ins = nc.tensor.matmul(b[:, pair * P:(pair + 1) * P], qkiT[rows, 2 + pair, :],
                                                   qkiT[rows, pair, :], start=True, stop=True)
                        ins.then_inc(dve_filled, 1)
                if part == 10:
                    for c in range(2):
                        b = fill_dve()
                        for pair in range(PAIRS):
                            ins = nc.tensor.matmul(b[:, pair * 2 * HD:(pair + 1) * 2 * HD], kdc[:, c, pair * P:(pair + 1) * P],
                                                   gla_in[:, i, W_COLS + pair * 2 * HD:W_COLS + (pair + 1) * 2 * HD],
                                                   start=True, stop=True)
                        ins.then_inc(dve_filled, 1)
                if part == 12:
                    pe.wait_ge(dve_emptied, read(k, "gla", 6 * i + 4))
                    b = fill_dve()
                    for h in range(HEADS):
                        nc.tensor.matmul(b[:, h * HD:(h + 1) * HD], a_intra[:, h, :],
                                         gla_in[:, i, W_COLS + h * HD:W_COLS + (h + 1) * HD],
                                         start=(h == 0), stop=False, skip_group_check=True)
                    for c in range(2):
                        toks = slice(c * GLA_CHUNK, (c + 1) * GLA_CHUNK)
                        for pair in range(PAIRS):
                            ins = nc.tensor.matmul(b[toks, pair * 2 * HD:(pair + 1) * 2 * HD], qkiT[:, pair, toks],
                                                   state[:, c, pair, :], start=False,
                                                   stop=(c == 1 and pair == PAIRS - 1), skip_group_check=True)
                    ins.then_inc(dve_filled, 1)

            def slot_v(c, s):
                if by_vector(s):
                    return
                tile, head = divmod(c, PH)
                n = c * SLOTS + s
                e = head * TOPK + s
                last = head == PH - 1 and v_count(c, s) == (c + 1) * V_PE
                if e == 0 and tile > 0:
                    pe.wait_ge(peer_added, tile)
                pe.wait_ge(v_landed[n % V_RING], 16 * (n // V_RING + 1))
                pe.wait_ge(diag_ready, v_count(c, s))
                for j in range(D // 512):
                    ins = nc.tensor.matmul(peer_acc[:, j * 512:(j + 1) * 512], diag[:, (v_count(c, s) - 1) % DIAGS, :],
                                           v_ring[:, n % V_RING, j * 512:(j + 1) * 512],
                                           start=(e == 0), stop=last)
                ins.then_inc(v_used, 1)

            interleave(front, lambda c, s: None, slot_v, lambda c: None)


_NAMES = ["x", "attn_norm_w", "w_in", "diff_q_norm_w", "diff_k_norm_w", "lambda_q1", "lambda_k1", "lambda_q2",
          "lambda_k2", "diff_out_norm_w", "gla_gate_w2", "gla_gate_b", "gla_out_norm_w", "w_out", "ffn_norm_w",
          "peer_w_q", "peer_sub_keys", "peer_u", "peer_v"]


def kernel(**inputs):
    import numpy as _np
    import concourse.bacc as _bacc
    from concourse import mybir as _mybir
    from concourse.bass_utils import run_bass_kernel_spmd as _run

    nc = _bacc.Bacc("TRN2", target_bir_lowering=False, num_devices=1, dynamic_dma_scratch_size=8192)
    arrays, args = {}, []
    for name in _NAMES:
        a = _np.asarray(inputs[name])
        if name == "peer_sub_keys":
            layers, heads, books, keys, width = a.shape
            a = a.transpose(0, 4, 1, 2, 3).reshape(layers, width, heads * books, keys)
        a = _np.ascontiguousarray(a)
        arrays[f"in_{name}"] = a
        args.append(nc.dram_tensor(f"in_{name}", a.shape, _mybir.dt.from_np(a.dtype), kind="ExternalInput").ap())
    shape = tuple(inputs["x"].shape)
    args.append(nc.dram_tensor("out_0", shape, _mybir.dt.float32, kind="ExternalOutput").ap())
    trunk(nc, *args)
    r = _run(nc, [arrays], core_ids=[0])
    return r.results[0]["out_0"]
```

```python
import math
from contextlib import ExitStack

import concourse.bass as bass
from concourse import mybir

F32 = mybir.dt.float32
U32 = mybir.dt.uint32
ALU = mybir.AluOpType
ACT = mybir.ActivationFunctionType
AX_X = mybir.AxisListType.X

P = 128
EPS = 1e-6
GLA_CHUNK = 64
GATE_NORMALIZER = 16.0
TOPK = 16
HALF = 2
W_COLS = 512
U_RING = 6
V_RING = 6
W_RING = 2
DIAGS = 4
ACT_BANKS = 3
DVE_BANKS = 3
V_EVERY = 8
LEAD = 10
LOWEST = -3.0e38
MASKED = -1.0e30


class Count:

    def __init__(self):
        self.n = {}

    def next(self, name):
        self.n[name] = self.n.get(name, 0) + 1
        return self.n[name]


def trunk(nc, x, attn_norm_w, w_in, q_norm_w, k_norm_w, lq1, lk1, lq2, lk2, diff_norm_w, gate_w2, gate_b,
          gla_norm_w, w_out, ffn_norm_w, w_q, keys_t, peer_u, peer_v, out):
    _, SEQ, D = x.shape
    LAYERS = w_in.shape[0]
    RANK, GK = gate_w2.shape[1:]
    HD = diff_norm_w.shape[1]
    DD = q_norm_w.shape[1]
    QH = D // 2
    HEADS = QH // HD
    GD = GK // HEADS
    PAIRS = HEADS // 2
    KC = D // P
    TILES = SEQ // P
    HALVES = TILES // HALF
    FRONTS = LAYERS * HALVES
    GROUPS = keys_t.shape[2]
    KEYS = keys_t.shape[3]
    PH = GROUPS // 2
    EXPERTS = peer_u.shape[1]
    PROJ_ORDER = (0, 1, 3, 2, 5, 4)
    PROJ = len(PROJ_ORDER)
    GPC = W_COLS // P
    CHUNKS = LAYERS * TILES * PH
    SLOTS = TOPK
    HPC = GPC // 2
    V_DVE = SLOTS // V_EVERY
    V_PE = SLOTS - V_DVE
    HTOK = HALF * P
    SMALL_LOADS = 16 * LAYERS * 11

    u_rows = peer_u.rearrange("l e d -> (l e) d")
    v_rows = peer_v.rearrange("l e d -> (l e) d")
    LAM_INIT = [0.8 - 0.6 * math.exp(-0.3 * l) for l in range(LAYERS)]

    NORM_PARTS = 5
    QK_AT = 2 * 2 * HALF - 1
    QK_FLIP_AT = QK_AT + 8
    LR_AT = QK_AT + 4
    ATTN_AT = QK_FLIP_AT + HALF + 1
    ATTN_STEP = 5
    ATTN_STEPS = HALF * HEADS // 2
    GLA_AT = (LR_AT + 2, LR_AT + 16)
    FINISH_AT = (ATTN_AT + 14, ATTN_AT + 24)
    MIX_AT = (ATTN_AT + 23, FINISH_AT[1] + 5)
    OUT_AT = tuple(p + 2 for p in MIX_AT)
    OUT_STEPS = 2 * D // W_COLS
    STATS_AT = tuple(p + OUT_STEPS for p in OUT_AT)
    MID_STEPS = STATS_AT[1] + 4
    PROJ_STEPS = 2 * PROJ * HALF
    ROUTE_TILE = 5
    ROUTE_STEP = HALF * ROUTE_TILE
    ROUTE_LEAD = 7
    QJ = GROUPS // GPC
    QS = GPC // 2 + HALF
    ROUTE_PARTS = QJ * ROUTE_STEP
    QUERY_AT = STATS_AT[1]
    SIL_AT = (7, 11)

    def product_at(p):
        if p < PROJ_STEPS:
            return ("in", *divmod(p // 2, HALF)) if p % 2 == 0 else None
        for i in range(HALF):
            if p in range(OUT_AT[i], OUT_AT[i] + OUT_STEPS, 2):
                return "out", (p - OUT_AT[i]) // 2, i
        return ("query", 0, 0) if p == QUERY_AT else None

    PRODUCT_PARTS = [2 * (product_at(p) is not None) for p in range(MID_STEPS)]
    PARTS = NORM_PARTS + MID_STEPS + sum(PRODUCT_PARTS) + ROUTE_PARTS
    PARTS_ALONE = PARTS - ROUTE_PARTS + ROUTE_TILE

    tiles = range(HALF)
    groups = [(2 * g, 0, "proj") for g in range(PROJ * HALF)] + [(LR_AT, 1, "lr")]
    groups += [(QK_FLIP_AT + i, 2, "qkT") for i in tiles for _ in range(2)]
    groups += [(ATTN_AT + ATTN_STEP * (s + 1), 3, "aT") for s in range(ATTN_STEPS) for _ in range(2)]
    groups += [(GLA_AT[i] + p, 4 + i, "gla") for i in tiles for p in (4, 4, 7)]
    groups += [(MIX_AT[i], 6, "mixT") for i in tiles for _ in range(2)]
    groups += [(STATS_AT[i] + 2, 7, "h2T") for i in tiles for _ in range(2)]
    groups += [(QUERY_AT, 0, "route"), (QUERY_AT + 2, 1, "route")]
    act_order = ["hT"] * 2 * HALF + [name for _, _, name in sorted(groups)] + ["route"] * (QS * QJ - 2)
    ACT_GROUPS = len(act_order)

    groups = [(OUT_AT[i] + 2 * j, 0, "out") for i in tiles for j in range(OUT_STEPS // 2)]
    groups += [(ATTN_AT + ATTN_STEP * s + h, 3, "attn") for s in range(ATTN_STEPS) for h in (0, 0, 1, 1)]
    groups += [(ATTN_AT + ATTN_STEP * (s + 1) + 2, 3, "attn") for s in range(ATTN_STEPS)]
    groups += [(GLA_AT[i] + p, 4 + i, "gla") for i in tiles for p in (0, 9, 9, 10, 12, 12)]
    dve_order = [name for _, _, name in sorted(groups)]
    DVE_GROUPS = len(dve_order)

    ATTN_DONE = tuple(min(4 * (s + 1), 4 * ATTN_STEPS) + s for s in (HEADS // 2, HEADS))

    def up_to(order, name, n):
        return [at for at, other in enumerate(order) if other == name][n - 1] + 1

    def queried(j):
        return QS * j + GPC // 2 if j else 3

    def scored(j, i):
        return QS * j + GPC // 2 + i + 1 if j else 2 * (i + 1)

    def read(k, name, n):
        return k * DVE_GROUPS + up_to(dve_order, name, n)

    def emptied(k, name, n):
        return k * ACT_GROUPS + up_to(act_order, name, n)

    with ExitStack() as ctx:
        def sb(name, shape, dt=F32):
            return ctx.enter_context(nc.sbuf_tensor(name, shape, dt))

        def sem(name):
            return ctx.enter_context(nc.semaphore(name))

        u_ring = sb("u_ring", [P, U_RING, D])
        v_ring = sb("v_ring", [P, V_RING, D])
        w_ring = sb("w_ring", [P, W_RING, KC, W_COLS])
        xs = sb("xs", [P, TILES, D])
        h2 = sb("h2", [P, TILES, D])
        hT = sb("hT", [P, KC, HTOK])
        mix = sb("mix", [P, HALF, D])
        h1 = mix
        work = sb("work", [P, 5 * D])
        dqk = work[:, 0:2 * D].rearrange("p (i c) -> p i c", i=HALF)
        gla_in = work[:, 2 * D:5 * D].rearrange("p (i c) -> p i c", i=HALF)
        probs = work[:, 0:2 * D].rearrange("p (m c) -> p m c", m=4)
        kT = sb("kT", [P, HEADS, SEQ])
        qT = sb("qT", [P, HEADS, HTOK])
        v_nat = sb("v_nat", [P, TILES, QH])
        hT_flat = hT[:, :, :].rearrange("p c t -> p (c t)")
        aT = hT_flat.rearrange("p (h c) -> p h c", h=HEADS)
        keysT = sb("keysT", [P, GROUPS, KEYS])
        norm_w = sb("norm_w", [P, 2, D])
        qk_w = sb("qk_w", [P, LAYERS, 2, DD])
        head_w = sb("head_w", [P, LAYERS, 2, HD])
        w_lr = sb("w_lr", [P, LAYERS, KC, RANK])
        w_gate = sb("w_gate", [RANK + 1, LAYERS, GK])
        lrT = sb("lrT", [RANK + 1, HTOK])
        lam_in = h2[:, TILES - 1, 0:4 * LAYERS * DD].rearrange("p (a l d) -> p a l d", a=4, l=LAYERS)
        lam_sum = sb("lam_sum", [P, 2, LAYERS])
        neg_lam = sb("neg_lam", [P, LAYERS])
        ident = sb("ident", [P, P])
        causal = sb("causal", [P, SEQ])
        tri = sb("tri", [P, P])
        suffix = sb("suffix", [P, P])
        in_chunk = sb("in_chunk", [P, 2])
        chunk_is = sb("chunk_is", [P, 2])
        iota = sb("iota", [P, TOPK])
        eps_c = sb("eps_c", [P, 1])
        one_c = sb("one_c", [P, 1])
        a_intra = sb("a_intra", [P, HEADS, P])
        gates_of = [(mix[:, i, QH:QH + GK], mix[:, i, QH + GK:D]) for i in range(HALF)]

        def gla_scratch(t0):
            flat = h2[:, t0:t0 + HALF, :].rearrange("p i d -> p (i d)")
            qd, ki, kdc, sil, qkiT = (flat[:, a:b] for a, b in (
                (0, GK), (GK, 2 * GK), (2 * GK, 4 * GK), (4 * GK, 4 * GK + QH), (4 * GK + QH, 2 * D)))
            return (qd, ki, kdc.rearrange("p (c k) -> p c k", c=2), sil,
                    qkiT.rearrange("p (a t) -> p a t", a=4))

        decay = sb("decay", [P, PAIRS, 2])
        state = sb("state", [P, 2, PAIRS, 2 * HD])
        square = sb("square", [P, D])
        sq = sb("sq", [P, 2 * 2 * HEADS * HALF])
        seed_ln = sb("seed_ln", [P, 2 * 2 * HEADS * HALF])
        seed = sb("seed", [P, 2 * 2 * HEADS * HALF])
        ms = sb("ms", [P, 2 * 2 * HEADS * HALF])
        rs = sb("rs", [P, 2 * 2 * HEADS * HALF])
        neg_max = sb("neg_max", [P, 4])
        row_sum = sb("row_sum", [P, 4])
        row_inv = sb("row_inv", [P, 4])
        qpT = work[:, 0:2 * GPC * HTOK].rearrange("p (b g c) -> p b g c", b=2, g=GPC)
        scores = mix[:, :, :].rearrange("p i (b g k) -> p i b g k", b=2, k=KEYS)
        free = [2 * GPC * HTOK]

        def scratch(n, dt=F32):
            free[0] += n
            ap = work[:, free[0] - n:free[0]]
            return ap if dt == F32 else ap.bitcast(dt)

        PICKS = HPC * TOPK
        top_s = scratch(GPC * TOPK).rearrange("p (g k) -> p g k", k=TOPK)
        top_i = scratch(GPC * TOPK, U32).rearrange("p (g k) -> p g k", k=TOPK)
        top_f = scratch(GPC * TOPK).rearrange("p (g k) -> p g k", k=TOPK)
        cand = scratch(PICKS * TOPK).rearrange("p (h k) -> p h k", h=HPC)
        best = scratch(PICKS).rearrange("p (h k) -> p h k", h=HPC)
        expo = scratch(PICKS).rearrange("p (h k) -> p h k", h=HPC)
        pos = scratch(PICKS, U32)
        pos_ij = scratch(2 * PICKS, U32).rearrange("p (a k) -> p a k", a=2)
        pos_f = scratch(2 * PICKS).rearrange("p (a k) -> p a k", a=2)
        sel = scratch(2 * PICKS).rearrange("p (a k) -> p a k", a=2)
        pick = scratch(PICKS * TOPK)
        gsum = sb("gsum", [P, HPC])
        gates = sb("gates", [P, TILES, PH, TOPK])
        experts = sb("experts", [P, TILES, PH * TOPK], U32)
        dots = sb("dots", [P, 2, SLOTS])
        acts = sb("acts", [P, 2, SLOTS])
        wts = sb("wts", [P, 2, SLOTS])
        diag = sb("diag", [P, DIAGS, P])

        peer_acc = ctx.enter_context(nc.psum_tensor("peer_acc", [P, D], F32))
        act_bank = [ctx.enter_context(nc.psum_tensor(f"act_bank{i}", [P, 512], F32)) for i in range(ACT_BANKS)]
        dve_bank = [ctx.enter_context(nc.psum_tensor(f"dve_bank{i}", [P, 512], F32)) for i in range(DVE_BANKS)]

        x_loaded = [sem(f"x_loaded{t}") for t in range(TILES)]
        small_loaded = sem("small_loaded")
        attn_w_loaded = sem("attn_w_loaded")
        ffn_w_loaded = sem("ffn_w_loaded")
        keys_loaded = sem("keys_loaded")
        w_loaded = [sem(f"w_loaded{i}") for i in range(W_RING)]
        u_landed = [sem(f"u_landed{i}") for i in range(U_RING)]
        v_landed = [sem(f"v_landed{i}") for i in range(V_RING)]
        stored = sem("stored")
        consts_ready = sem("consts_ready")
        pool_step = sem("pool_step")
        act_step = sem("act_step")
        dve_step = sem("dve_step")
        prep_ready = sem("prep_ready")
        lam_exp = sem("lam_exp")
        act_filled = sem("act_filled")
        act_emptied = sem("act_emptied")
        dve_filled = sem("dve_filled")
        dve_emptied = sem("dve_emptied")
        sums_ready = sem("sums_ready")
        seed_ready = sem("seed_ready")
        squares_ready = sem("squares_ready")
        h1_ready = sem("h1_ready")
        h2_ready = sem("h2_ready")
        qk_ready = sem("qk_ready")
        scores_ready = sem("scores_ready")
        exp_ready = sem("exp_ready")
        a_ready = sem("a_ready")
        soft_ready = sem("soft_ready")
        g_ready = sem("g_ready")
        gla_ready = sem("gla_ready")
        silu_ready = sem("silu_ready")
        mix_ready = sem("mix_ready")
        gate_arg = sem("gate_arg")
        gate_exp = sem("gate_exp")
        routed = sem("routed")
        u_used = sem("u_used")
        act_ready = sem("act_ready")
        wts_ready = sem("wts_ready")
        diag_ready = sem("diag_ready")
        v_used = sem("v_used")
        v_added = sem("v_added")
        peer_added = sem("peer_added")

        block = ctx.enter_context(nc.Block())

        def by_vector(s):
            return s % V_EVERY == V_EVERY - 1

        def v_count(c, s):
            mine = s // V_EVERY + 1
            return c * V_DVE + mine if by_vector(s) else c * V_PE + s + 1 - s // V_EVERY

        def interleave(front, slot_u, slot_v, begin):
            parts = (None for k in range(FRONTS) for _ in front(k))
            for _ in range(PARTS_ALONE):
                next(parts)
            for s in range(SLOTS):
                slot_u(0, s)
            done = 0
            for n in range(CHUNKS * SLOTS):
                c, s = divmod(n, SLOTS)
                if c + 1 < CHUNKS:
                    slot_u(c + 1, s)
                if s == 0:
                    begin(c)
                due = min(n + 1, LEAD) + (n + 1) * PARTS // (HALF * PH * SLOTS)
                for _ in range(due - done):
                    next(parts, None)
                done = due
                slot_v(c, s)

        @block.sync
        def _(sp):
            def load_x(t0):
                for t in range(t0, t0 + HALF):
                    sp.dma_start(xs[:, t, :], x[0, t * P:(t + 1) * P, :]).then_inc(x_loaded[t], 16)

            load_x(0)
            sp.dma_start(norm_w[:, 0, :], attn_norm_w[0].partition_broadcast(P)).then_inc(attn_w_loaded, 16)

            used = []

            def load_w(n, source):
                if n >= W_RING:
                    sp.wait_ge(*used[n - W_RING])
                sp.dma_start(w_ring[:, n % W_RING], source).then_inc(w_loaded[n % W_RING], 16)

            n = 0
            for k in range(FRONTS):
                l = k // HALVES
                w_in_v = w_in[l].rearrange("(c p) n -> p c n", p=P)
                w_out_v = w_out[l].rearrange("(c p) n -> p c n", p=P)
                w_q_v = w_q[l].rearrange("(c p) n -> p c n", p=P)
                sources = [w_in_v[:, :, j * W_COLS:(j + 1) * W_COLS] for j in PROJ_ORDER]
                sources += [w_out_v[:, :, j * W_COLS:(j + 1) * W_COLS] for j in range(D // W_COLS)]
                sources += [w_q_v[:, :, j * W_COLS:(j + 1) * W_COLS] for j in range(GROUPS // GPC)]
                used += [(act_filled, emptied(k, "proj", HALF * (j + 1))) for j in range(PROJ)]
                used += [(dve_filled, read(k, "out", D // W_COLS + j + 1)) for j in range(D // W_COLS)]
                used += [(act_filled, emptied(k, "route", queried(j))) for j in range(QJ)]
                for j, source in enumerate(sources):
                    load_w(n, source)
                    n += 1
                    if k % HALVES == HALVES - 1 and l + 1 < LAYERS and j == 2:
                        sp.wait_ge(h1_ready, HALF * (k + 1))
                        sp.dma_start(norm_w[:, 0, :], attn_norm_w[l + 1].partition_broadcast(P)).then_inc(attn_w_loaded, 16)
                    if k % HALVES == 0 and l > 0 and j == 2:
                        sp.wait_ge(h2_ready, HALF * k)
                        sp.dma_start(norm_w[:, 1, :], ffn_norm_w[l].partition_broadcast(P)).then_inc(ffn_w_loaded, 16)
                        sp.wait_ge(act_filled, ACT_GROUPS * k)
                        sp.dma_start(keysT[:], keys_t[l]).then_inc(keys_loaded, 16)
                    if k == 0 and j == 1:
                        small = 0
                        for ll in range(LAYERS):
                            loads = [
                                (qk_w[:, ll, 0, :], q_norm_w[ll].partition_broadcast(P)),
                                (qk_w[:, ll, 1, :], k_norm_w[ll].partition_broadcast(P)),
                                (head_w[:, ll, 0, :], diff_norm_w[ll].partition_broadcast(P)),
                                (head_w[:, ll, 1, :], gla_norm_w[ll].partition_broadcast(P)),
                                (w_lr[:, ll], w_in[ll, :, PROJ * W_COLS:].rearrange("(c p) n -> p c n", p=P)),
                                (w_gate[0:RANK, ll, :], gate_w2[ll]),
                                (w_gate[RANK:RANK + 1, ll, :], gate_b[ll:ll + 1, :]),
                            ]
                            loads += [(lam_in[:, a, ll, :], v[ll].partition_broadcast(P))
                                      for a, v in enumerate((lq1, lk1, lq2, lk2))]
                            for to, of in loads:
                                sp.dma_start(to, of).then_inc(small_loaded, 16)
                                small += 16
                        assert small == SMALL_LOADS
                        sp.dma_start(norm_w[:, 1, :], ffn_norm_w[0].partition_broadcast(P)).then_inc(ffn_w_loaded, 16)
                        sp.dma_start(keysT[:], keys_t[0]).then_inc(keys_loaded, 16)
                        for t0 in range(HALF, TILES, HALF):
                            load_x(t0)
            for t in range(TILES):
                sp.wait_ge(peer_added, (LAYERS - 1) * TILES + t + 1)
                sp.dma_start(out[0, t * P:(t + 1) * P, :], xs[:, t, :]).then_inc(stored, 16)
            sp.wait_ge(stored, 16 * TILES)

        @block.gpsimd
        def _(pool):
            count = Count()

            def link(ins):
                ins.then_inc(pool_step, 1)
                pool.wait_ge(pool_step, count.next("step"))

            def keep(ap, op, base, mult, pattern, fill):
                link(pool.affine_select(out=ap, in_=ap, compare_op=op, fill=fill, base=base,
                                        pattern=pattern, channel_multiplier=mult))

            link(pool.memset(ident[:], 0.0))
            keep(ident[:], ALU.not_equal, 0, 1, [[-1, P]], 1.0)
            link(pool.memset(eps_c[:], EPS))
            link(pool.memset(one_c[:], 1.0))
            link(pool.memset(lrT[:], 1.0))
            link(pool.memset(causal[:], 0.0))
            keep(causal[:, SEQ - P:], ALU.is_ge, 0, 1, [[-1, P]], MASKED)
            link(pool.memset(tri[:], 1.0 / GATE_NORMALIZER))
            keep(tri[:], ALU.is_ge, 0, -1, [[1, P]], 0.0)
            link(pool.memset(tri[0:GLA_CHUNK, GLA_CHUNK:P], 0.0))
            link(pool.memset(suffix[:], 1.0 / GATE_NORMALIZER))
            keep(suffix[:], ALU.is_gt, 0, 1, [[-1, P]], 0.0)
            link(pool.memset(suffix[GLA_CHUNK:P, 0:GLA_CHUNK], 0.0))
            link(pool.memset(in_chunk[:], 0.0))
            link(pool.memset(in_chunk[0:GLA_CHUNK, 0:1], 1.0 / GATE_NORMALIZER))
            link(pool.memset(in_chunk[GLA_CHUNK:P, 1:2], 1.0 / GATE_NORMALIZER))
            link(pool.memset(chunk_is[:], 0.0))
            link(pool.memset(chunk_is[0:GLA_CHUNK, 0:1], 1.0))
            link(pool.memset(chunk_is[GLA_CHUNK:P, 1:2], 1.0))
            link(pool.memset(a_intra[:], 0.0))
            link(pool.memset(state[:], 0.0))
            pool.iota(iota[:], [[1, TOPK]], base=0, channel_multiplier=0,
                      allow_small_or_imprecise_dtypes=True).then_inc(consts_ready, 1)

            def gather(table, ring, depth, landed, c, s):
                n = c * SLOTS + s
                tile, head = divmod(c, PH)
                e = head * TOPK + s
                pool.indirect_dma_start(
                    ring[:, n % depth, :], None, table,
                    bass.IndirectOffsetOnAxis(ap=experts[:, tile % TILES, e:e + 1], axis=0),
                ).then_inc(landed[n % depth], 16)

            for c in range(-1, CHUNKS):
                if c + 1 < CHUNKS and (c + 1) % HPC == 0:
                    k, part = divmod(c + 1, HALF * PH)
                    i, head = divmod(part, PH)
                    pool.wait_ge(routed, (k * QJ + head // HPC) * HALF + i + 1)
                for s in range(SLOTS):
                    if c + 1 < CHUNKS:
                        n = (c + 1) * SLOTS + s
                        if n >= U_RING:
                            pool.wait_ge(u_used, n - U_RING + 1)
                        gather(u_rows, u_ring, U_RING, u_landed, c + 1, s)
                    if c >= 0:
                        n = c * SLOTS + s
                        if n >= V_RING:
                            old_c, old_s = divmod(n - V_RING, SLOTS)
                            pool.wait_ge(v_added if by_vector(old_s) else v_used, v_count(old_c, old_s))
                        gather(v_rows, v_ring, V_RING, v_landed, c, s)

        @block.scalar
        def _(act):
            count = Count()

            def link(ins):
                ins.then_inc(act_step, 1)
                act.wait_ge(act_step, count.next("step"))

            def bank():
                n = count.next("bank")
                act.wait_ge(act_filled, n)
                return act_bank[(n - 1) % ACT_BANKS]

            def empty(to, cols=512, rows=P):
                b = bank()
                nc.scalar.activation(to, b[0:rows, 0:cols], ACT.Copy).then_inc(act_emptied, 1)

            def rsqrt_seed(cols, width):
                link(nc.scalar.activation(seed_ln[:, cols], sq[:, cols], ACT.Ln, bias=eps_c[:], scale=1.0 / width))
                nc.scalar.activation(seed[:, cols], seed_ln[:, cols], ACT.Exp, scale=-0.5).then_inc(seed_ready, 1)

            def stats(t, i):
                link(nc.scalar.activation(square[:], xs[:, t, :], ACT.Square, accum_out=sq[:, i:i + 1]))
                rsqrt_seed(slice(i, i + 1), D)

            def empty_hT(i):
                for g in range(2):
                    empty(hT[:, 4 * g:4 * g + 4, i * P:(i + 1) * P])

            act.wait_ge(consts_ready, 1)

            def front(k):
                l, t0 = k // HALVES, (k % HALVES) * HALF
                for p in range(NORM_PARTS):
                    if p < HALF:
                        if l == 0:
                            act.wait_ge(x_loaded[t0 + p], 16)
                        else:
                            act.wait_ge(peer_added, (l - 1) * TILES + t0 + p + 1)
                        stats(t0 + p, p)
                    if p >= 3:
                        empty_hT(p - 3)
                    yield
                for p in range(MID_STEPS):
                    j, i = divmod(p // 2, HALF)
                    if p == 1 and k:
                        act.wait_ge(routed, k * QJ * HALF)
                    if p % 2 == 1 and j < PROJ:
                        source = PROJ_ORDER[j]
                        if source < 2:
                            empty(dqk[:, i, source * QH:(source + 1) * QH])
                        elif source == 2:
                            empty(v_nat[:, t0 + i, :])
                        else:
                            empty(gla_in[:, i, (source - 3) * W_COLS:(source - 2) * W_COLS])
                    if p == QUERY_AT + 1:
                        empty(qpT[:, 0, :, 0:P])
                    for _ in range(PRODUCT_PARTS[p]):
                        yield
                    if p == QUERY_AT + 3:
                        empty(scores[:, 0, 0])
                    if p == LR_AT + 1:
                        empty(lrT[0:RANK, :], HTOK, RANK)
                    i = p - QK_FLIP_AT - 1
                    if 0 <= i < HALF:
                        empty(qT[:, :, i * P:(i + 1) * P])
                        empty(kT[:, :, (t0 + i) * P:(t0 + i + 1) * P])
                    if p in (QK_AT + 1, QK_AT + 3):
                        i = (p - QK_AT) // 2
                        if i:
                            act.wait_ge(sums_ready, count.next("sums"))
                        act.wait_ge(act_emptied, emptied(k, "proj", 2 * HALF))
                        nc.scalar.activation(square[:], dqk[:, i, :], ACT.Square).then_inc(squares_ready, 1)
                    if p == QK_AT + 5:
                        act.wait_ge(sums_ready, count.next("sums"))
                        rsqrt_seed(slice(0, HALF * 4 * HEADS), DD)
                    if p == QK_AT + 6 and k == 0:
                        act.wait_ge(prep_ready, 1)
                        nc.scalar.activation(lam_sum[:], lam_sum[:], ACT.Exp).then_inc(lam_exp, 1)
                    attend(t0, p - ATTN_AT)
                    for i in range(HALF):
                        linear(k, t0, i, p - GLA_AT[i])
                    for i in range(HALF):
                        finish(k, i, p - FINISH_AT[i])
                        if p == MIX_AT[i] + 1:
                            empty_hT(i)
                        if p == STATS_AT[i]:
                            act.wait_ge(dve_emptied, read(k, "out", D // W_COLS * (i + 1)))
                            stats(t0 + i, i)
                        if p == STATS_AT[i] + 3:
                            empty_hT(i)
                    yield
                for p in range(ROUTE_PARTS):
                    if p == 2:
                        empty(qpT[:, 0, :, P:2 * P])
                    if p == 4:
                        empty(scores[:, 1, 0])
                    j, part = divmod(p + ROUTE_LEAD, ROUTE_STEP)
                    if 0 < j < QJ and part in (2, 4):
                        empty(qpT[:, j % 2, part - 2:part, :])
                    if 0 < j < QJ and part == 6:
                        if j >= 2:
                            act.wait_ge(routed, (k * QJ + j - 1) * HALF)
                        for i in range(HALF):
                            empty(scores[:, i, j % 2])
                    n, part = divmod(p, ROUTE_TILE)
                    if part == 3:
                        act.wait_ge(gate_arg, k * QJ * HALF + n + 1)
                        nc.scalar.activation(expo, expo, ACT.Exp).then_inc(gate_exp, 1)
                    yield

            def attend(t0, at):
                step, part = divmod(at, ATTN_STEP)
                if part == 1 and 0 < step <= ATTN_STEPS:
                    i, hg = divmod(step - 1, HEADS // 2)
                    keys = (t0 + i + 1) * P
                    for h in (2 * hg, 2 * hg + 1):
                        empty(aT[:, h, 0:keys], keys)
                if part == 3 and 0 <= step < ATTN_STEPS:
                    keys = (t0 + step // (HEADS // 2) + 1) * P
                    act.wait_ge(scores_ready, count.next("scores"))
                    for m in range(4):
                        ins = nc.scalar.activation(probs[:, m, 0:keys], probs[:, m, 0:keys], ACT.Exp,
                                                   bias=neg_max[:, m:m + 1], accum_out=row_sum[:, m:m + 1])
                    ins.then_inc(exp_ready, 1)

            def linear(k, t0, i, part):
                qd, ki, kdc, sil, qkiT = gla_scratch(t0)
                g_log = gates_of[i][1]
                if part == 2:
                    act.wait_ge(dve_emptied, read(k, "gla", 6 * i + 1))
                    link(nc.scalar.activation(g_log, g_log, ACT.Exp, scale=-1.0))
                    nc.scalar.activation(g_log, g_log, ACT.Ln, bias=one_c[:]).then_inc(soft_ready, 1)
                if part == 5:
                    b = bank()
                    nc.scalar.activation(qd, b[:, 0:GK], ACT.Exp)
                    nc.scalar.activation(ki, b[:, 0:GK], ACT.Exp, scale=-1.0)
                    nc.scalar.activation(kdc[:, 0, :], b[:, GK:2 * GK], ACT.Exp).then_inc(act_emptied, 1)
                    b = bank()
                    nc.scalar.activation(decay[:].rearrange("p a c -> p (a c)"), b[:, 0:4],
                                         ACT.Exp).then_inc(act_emptied, 1)
                if part == 8:
                    empty(qkiT)
                if part == SIL_AT[i]:
                    act.wait_ge(act_emptied, emptied(k, "proj", HALF * (PROJ - 1)))
                    if i:
                        act.wait_ge(mix_ready, k * HALF + i)
                    nc.scalar.activation(sil, gla_in[:, i, 2 * W_COLS:3 * W_COLS], ACT.Exp,
                                         scale=-1.0).then_inc(silu_ready, 1)

            def finish(k, i, part):
                if part == 0:
                    act.wait_ge(dve_emptied, max(read(k, "gla", 6 * (i + 1)),
                                                 read(k, "attn", ATTN_DONE[i])))
                    nc.scalar.activation(square[:], mix[:, i, :], ACT.Square).then_inc(squares_ready, 1)
                if part == 2:
                    act.wait_ge(sums_ready, count.next("sums"))
                    rsqrt_seed(slice(0, 2 * HEADS), HD)

            def begin(c):
                act.wait_ge(u_used, (c + 1) * SLOTS)
                nc.scalar.activation(acts[:, c % 2, :], dots[:, c % 2, :], ACT.Gelu).then_inc(act_ready, 1)

            def slot_v(c, s):
                if s == 0:
                    act.wait_ge(wts_ready, c + 1)
                if by_vector(s):
                    return
                n = v_count(c, s) - 1
                if n >= DIAGS:
                    act.wait_ge(v_used, n - DIAGS + 1)
                nc.scalar.activation(diag[:, n % DIAGS, :], ident[:], ACT.Copy,
                                     scale=wts[:, c % 2, s:s + 1]).then_inc(diag_ready, 1)

            interleave(front, lambda c, s: None, slot_v, begin)

        @block.vector
        def _(dve):
            count = Count()

            def link(ins):
                ins.then_inc(dve_step, 1)
                dve.wait_ge(dve_step, count.next("step"))

            def tell(ins, sem, name):
                ins.then_inc(sem, 1)
                dve.wait_ge(sem, count.next(name))

            def bank():
                n = count.next("bank")
                dve.wait_ge(dve_filled, n)
                return dve_bank[(n - 1) % DVE_BANKS]

            def release(ins):
                tell(ins, dve_emptied, "emptied")

            def rsqrt(cols, width):
                dve.wait_ge(seed_ready, count.next("seed"))
                nc.vector.tensor_scalar(ms[:, cols], sq[:, cols], 1.0 / width, EPS, ALU.mult, ALU.add)
                link(nc.vector.tensor_tensor(rs[:, cols], seed[:, cols], seed[:, cols], ALU.mult))
                link(nc.vector.tensor_tensor(rs[:, cols], rs[:, cols], ms[:, cols], ALU.mult))
                link(nc.vector.tensor_scalar(rs[:, cols], rs[:, cols], -0.5, 1.5, ALU.mult, ALU.add))
                link(nc.vector.tensor_tensor(rs[:, cols], rs[:, cols], seed[:, cols], ALU.mult))

            def norm(to, t, i, weight, ready, name):
                rsqrt(slice(i, i + 1), D)
                tell(nc.vector.scalar_tensor_tensor(out=to, in0=xs[:, t, :], scalar=rs[:, i:i + 1], in1=weight,
                                                    op0=ALU.mult, op1=ALU.mult), ready, name)

            def over(ap, n, w):
                return ap.unsqueeze(2).to_broadcast([P, n, w])

            def each(ap, n, w):
                return ap.unsqueeze(1).to_broadcast([P, n, w])

            def prepare():
                dve.wait_ge(small_loaded, SMALL_LOADS)
                for a in range(2):
                    link(nc.vector.tensor_tensor(lam_in[:, 2 * a], lam_in[:, 2 * a], lam_in[:, 2 * a + 1], ALU.mult))
                    ins = nc.vector.tensor_reduce(lam_sum[:, a, :], lam_in[:, 2 * a], op=ALU.add, axis=AX_X)
                    if a == 0:
                        link(ins)
                ins.then_inc(prep_ready, 1)
                for l in range(LAYERS):
                    link(nc.vector.tensor_scalar_mul(qk_w[:, l, 0, :], qk_w[:, l, 0, :], DD ** -0.5))
                    link(nc.vector.tensor_scalar_mul(head_w[:, l, 0, :], head_w[:, l, 0, :], 1.0 - LAM_INIT[l]))

            dve.wait_ge(consts_ready, 1)

            def first8(values, tops, index, n):
                for g in range(n):
                    ins = nc.vector.max(tops[:, g, 0:8], values[:, g, :])
                link(ins)
                for g in range(n):
                    nc.vector.max_index(index[:, g, 0:8], tops[:, g, 0:8], values[:, g, :])
                for g in range(n):
                    ins = nc.vector.match_replace(values[:, g, :], tops[:, g, 0:8], values[:, g, :], LOWEST)
                link(ins)

            def next8(values, tops, index, n):
                for g in range(n):
                    ins = nc.vector.max(tops[:, g, 8:16], values[:, g, :])
                link(ins)
                for g in range(n):
                    ins = nc.vector.max_index(index[:, g, 8:16], tops[:, g, 8:16], values[:, g, :])
                link(ins)

            def front(k):
                l, t0 = k // HALVES, (k % HALVES) * HALF
                n = 4 * HEADS
                dve.wait_ge(attn_w_loaded, 16 * (l + 1))
                for p in range(NORM_PARTS):
                    if 1 <= p <= HALF:
                        norm(h1[:, p - 1, :], t0 + p - 1, p - 1, norm_w[:, 0, :], h1_ready, "h1")
                    yield
                if k % HALVES == 0 and l > 0:
                    link(nc.vector.memset(state[:, 0], 0.0))
                if k == 0:
                    prepare()
                for p in range(MID_STEPS):
                    for i in range(HALF):
                        j, odd = divmod(p - OUT_AT[i] - 1, 2)
                        if 0 <= j < D // W_COLS and not odd:
                            b = bank()
                            v = xs[:, t0 + i, j * W_COLS:(j + 1) * W_COLS]
                            release(nc.vector.tensor_tensor(v, v, b[:], ALU.add))
                    for _ in range(PRODUCT_PARTS[p]):
                        yield
                    if p in (QK_AT + 2, QK_AT + 4):
                        i = (p - QK_AT) // 2 - 1
                        dve.wait_ge(squares_ready, count.next("squares"))
                        tell(nc.vector.tensor_reduce(sq[:, i * n:(i + 1) * n],
                                                     square[:].rearrange("p (g d) -> p g d", d=DD),
                                                     op=ALU.add, axis=AX_X), sums_ready, "sums")
                    if p == QK_AT + 6:
                        rsqrt(slice(0, HALF * n), DD)
                    if p in (QK_AT + 7, QK_AT + 8):
                        i = p - QK_AT - 7
                        v = dqk[:, i, :].rearrange("p (g d) -> p g d", d=DD)
                        link(nc.vector.tensor_tensor(v, v, over(rs[:, i * n:(i + 1) * n], n, DD), ALU.mult))
                        for j in range(2):
                            v = dqk[:, i, j * QH:(j + 1) * QH].rearrange("p (g d) -> p g d", d=DD)
                            ins = nc.vector.tensor_tensor(v, v, each(qk_w[:, l, j, :], 2 * HEADS, DD), ALU.mult)
                            if j == 0:
                                link(ins)
                            else:
                                tell(ins, qk_ready, "qk")
                    if p == QK_AT + 9 and k == 0:
                        dve.wait_ge(lam_exp, 1)
                        link(nc.vector.tensor_tensor(neg_lam[:], lam_sum[:, 1, :], lam_sum[:, 0, :], ALU.subtract))
                        for ll in range(LAYERS):
                            link(nc.vector.tensor_scalar_add(neg_lam[:, ll:ll + 1], neg_lam[:, ll:ll + 1],
                                                             -LAM_INIT[ll]))
                    attend(k, l, t0, p - ATTN_AT)
                    for i in range(HALF):
                        linear(k, t0, i, p - GLA_AT[i])
                    for i in range(HALF):
                        finish(l, t0, i, p - FINISH_AT[i])
                        if p == STATS_AT[i] + 1:
                            dve.wait_ge(ffn_w_loaded, 16 * (l + 1))
                            norm(h2[:, t0 + i, :], t0 + i, i, norm_w[:, 1, :], h2_ready, "h2")
                    yield
                for p in range(ROUTE_PARTS):
                    n, part = divmod(p, ROUTE_TILE)
                    j, i = divmod(n, HALF)
                    route(k, l, t0, i, j, part)
                    yield

            def attend(k, l, t0, at):
                step, part = divmod(at, ATTN_STEP)
                keys = (t0 + step // (HEADS // 2) + 1) * P
                now = 0 <= step < ATTN_STEPS
                if at == 1:
                    dve.wait_ge(act_emptied, emptied(k, "qkT", 2 * HALF))
                if part in (1, 2) and now:
                    for m in (2 * part - 2, 2 * part - 1):
                        b = bank()
                        release(nc.vector.tensor_tensor(probs[:, m, 0:keys], b[:, 0:keys],
                                                        causal[:, SEQ - keys:], ALU.add))
                    if part == 2:
                        tell(nc.vector.tensor_reduce(neg_max[:], probs[:, :, 0:keys], op=ALU.max, axis=AX_X,
                                                     negate=True), scores_ready, "scores")
                if part == 3 and 0 < step <= ATTN_STEPS:
                    i, hg = divmod(step - 1, HEADS // 2)
                    b = bank()
                    release(nc.vector.tensor_copy(mix[:, i, hg * 2 * HD:(hg + 1) * 2 * HD], b[:, 0:2 * HD]))
                if part == 4 and now:
                    dve.wait_ge(exp_ready, count.next("exp"))
                    link(nc.vector.reciprocal(row_inv[:], row_sum[:]))
                    for h in range(2):
                        link(nc.vector.tensor_tensor(row_inv[:, 2 * h + 1:2 * h + 2], row_inv[:, 2 * h + 1:2 * h + 2],
                                                     neg_lam[:, l:l + 1], ALU.mult))
                        link(nc.vector.tensor_scalar(probs[:, 2 * h, 0:keys], probs[:, 2 * h, 0:keys],
                                                     row_inv[:, 2 * h:2 * h + 1], None, ALU.mult))
                        ins = nc.vector.scalar_tensor_tensor(
                            out=probs[:, 2 * h, 0:keys], in0=probs[:, 2 * h + 1, 0:keys],
                            scalar=row_inv[:, 2 * h + 1:2 * h + 2], in1=probs[:, 2 * h, 0:keys],
                            op0=ALU.mult, op1=ALU.add)
                        if h == 0:
                            link(ins)
                    tell(ins, a_ready, "a")

            def linear(k, t0, i, part):
                qd, ki, kdc, sil, _ = gla_scratch(t0)
                z, g_log = gates_of[i]
                if part == 1:
                    b = bank()
                    link(nc.vector.tensor_scalar(z, b[:, 0:GK], 0.0, None, ALU.min))
                    release(nc.vector.scalar_tensor_tensor(out=g_log, in0=z, scalar=-2.0, in1=b[:, 0:GK],
                                                           op0=ALU.mult, op1=ALU.add))
                if part == 3:
                    dve.wait_ge(soft_ready, count.next("soft"))
                    tell(nc.vector.tensor_tensor(g_log, z, g_log, ALU.subtract), g_ready, "g")
                if part == 6:
                    dve.wait_ge(act_emptied, emptied(k, "gla", 3 * i + 2))
                    for c in (1, 0):
                        link(nc.vector.scalar_tensor_tensor(out=kdc[:, c, :], in0=kdc[:, 0, :],
                                                            scalar=chunk_is[:, c:c + 1], in1=gla_in[:, i, GK:2 * GK],
                                                            op0=ALU.mult, op1=ALU.mult))
                    link(nc.vector.tensor_tensor(ki, ki, gla_in[:, i, GK:2 * GK], ALU.mult))
                    tell(nc.vector.scalar_tensor_tensor(out=qd, in0=gla_in[:, i, 0:GK], scalar=GD ** -0.5,
                                                        in1=qd, op0=ALU.mult, op1=ALU.mult), gla_ready, "gla")
                if part == 10:
                    mask = tri[:].bitcast(U32).unsqueeze(1).to_broadcast([P, 2, P])
                    for b2 in range(2):
                        b = bank()
                        release(nc.vector.copy_predicated(
                            a_intra[:].rearrange("p (h b) i -> p b h i", b=2)[:, b2], mask,
                            b[:, 0:2 * P].rearrange("p (h i) -> p h i", h=2)))
                if part in (11, 13):
                    c = (part - 11) // 2
                    b = bank()
                    if c == 1:
                        dve.wait_ge(dve_filled, count.n["bank"] + 1)
                    for pair in range(PAIRS):
                        for s in range(2):
                            rows = slice(s * GD, (s + 1) * GD)
                            cols = slice(s * HD, (s + 1) * HD)
                            ins = nc.vector.scalar_tensor_tensor(
                                out=state[rows, (c + 1) % 2, pair, cols], in0=state[rows, c, pair, cols],
                                scalar=decay[rows, pair, c:c + 1],
                                in1=b[rows, pair * 2 * HD + s * HD:pair * 2 * HD + (s + 1) * HD],
                                op0=ALU.mult, op1=ALU.add)
                    release(ins)
                if part == 13:
                    b = bank()
                    release(nc.vector.tensor_copy(mix[:, i, QH:D], b[:]))
                    link(nc.vector.tensor_tensor(sil, sil, gla_in[:, i, 2 * W_COLS:3 * W_COLS], ALU.mult))
                if part == SIL_AT[i] + 1:
                    dve.wait_ge(silu_ready, count.next("silu"))
                    link(nc.vector.tensor_scalar_add(sil, sil, 1.0))
                    link(nc.vector.reciprocal(sil, sil))

            def finish(l, t0, i, part):
                sil = gla_scratch(t0)[3]
                if part == 1:
                    dve.wait_ge(squares_ready, count.next("squares"))
                    tell(nc.vector.tensor_reduce(sq[:, 0:2 * HEADS], square[:].rearrange("p (g d) -> p g d", d=HD),
                                                 op=ALU.add, axis=AX_X), sums_ready, "sums")
                if part == 3:
                    rsqrt(slice(0, 2 * HEADS), HD)
                    m = mix[:, i, :].rearrange("p (g d) -> p g d", d=HD)
                    link(nc.vector.tensor_tensor(m, m, over(rs[:, 0:2 * HEADS], 2 * HEADS, HD), ALU.mult))
                if part == 4:
                    m = mix[:, i, :].rearrange("p (a h d) -> p a h d", a=2, d=HD)
                    hw = head_w[:, l].unsqueeze(2).to_broadcast([P, 2, HEADS, HD])
                    link(nc.vector.tensor_tensor(m, m, hw, ALU.mult))
                    tell(nc.vector.tensor_tensor(mix[:, i, QH:D], mix[:, i, QH:D], sil, ALU.mult), mix_ready, "mix")

            def route(k, l, t0, i, j, part):
                t, heads = t0 + i, slice(j * HPC, (j + 1) * HPC)
                square_of = [P, HPC, TOPK, TOPK]
                best_pos = pos.rearrange("p (h k) -> p h k", h=HPC)
                fs = top_f.rearrange("p (h c) k -> p h c k", c=2)
                flat = pick.rearrange("p (n a) -> p n a", a=TOPK)
                four = pick.rearrange("p (h n a) -> p h n a", h=HPC, a=TOPK)

                def looked_up(c):
                    link(nc.vector.tensor_tensor(flat, over(pos_f[:, c, :], PICKS, TOPK),
                                                 each(iota[:], PICKS, TOPK), ALU.is_equal))
                    link(nc.vector.tensor_tensor(four, four, fs[:, :, c, :].unsqueeze(2).to_broadcast(square_of),
                                                 ALU.mult))
                    link(nc.vector.tensor_reduce(sel[:, c, :], flat, op=ALU.add, axis=AX_X))

                if part == 0:
                    dve.wait_ge(act_emptied, emptied(k, "route", scored(j, i)))
                    first8(scores[:, i, j % 2], top_s, top_i, GPC)
                if part == 1:
                    next8(scores[:, i, j % 2], top_s, top_i, GPC)
                    link(nc.vector.tensor_copy(top_f, top_i))
                    tops = top_s.rearrange("p (h c) k -> p h c k", c=2)
                    link(nc.vector.tensor_tensor(cand.rearrange("p h (a b) -> p h a b", b=TOPK),
                                                 tops[:, :, 0, :].unsqueeze(3).to_broadcast(square_of),
                                                 tops[:, :, 1, :].unsqueeze(2).to_broadcast(square_of), ALU.add))
                if part == 2:
                    first8(cand, best, best_pos, HPC)
                    next8(cand, best, best_pos, HPC)
                    tell(nc.vector.tensor_tensor(expo, best, over(best[:, :, 0], HPC, TOPK), ALU.subtract),
                         gate_arg, "gate_arg")
                if part == 3:
                    nc.vector.tensor_scalar(pos_ij[:, 0, :], pos, 4, None, ALU.logical_shift_right)
                    link(nc.vector.tensor_scalar(pos_ij[:, 1, :], pos, TOPK - 1, None, ALU.bitwise_and))
                    link(nc.vector.tensor_copy(pos_f, pos_ij))
                    looked_up(0)
                if part == 4:
                    looked_up(1)
                    dve.wait_ge(gate_exp, (k * QJ + j) * HALF + i + 1)
                    link(nc.vector.tensor_reduce(gsum[:], expo, op=ALU.add, axis=AX_X))
                    link(nc.vector.reciprocal(gsum[:], gsum[:]))
                    link(nc.vector.tensor_tensor(gates[:, t, heads], expo, over(gsum[:], HPC, TOPK), ALU.mult))
                    link(nc.vector.scalar_tensor_tensor(out=sel[:, 0, :], in0=sel[:, 0, :], scalar=float(KEYS),
                                                        in1=sel[:, 1, :], op0=ALU.mult, op1=ALU.add))
                    tell(nc.vector.tensor_scalar_add(experts[:, t, j * PICKS:(j + 1) * PICKS], sel[:, 0, :],
                                                     float(l * EXPERTS)), routed, "routed")

            def add_tile(tile):
                dve.wait_ge(v_used, (tile + 1) * PH * V_PE)
                v = xs[:, tile % TILES, :]
                tell(nc.vector.tensor_tensor(v, v, peer_acc[:], ALU.add), peer_added, "peer_added")

            def begin(c):
                if c % PH == 0 and c > 0:
                    add_tile(c // PH - 1)
                tile, head = divmod(c, PH)
                dve.wait_ge(act_ready, c + 1)
                tell(nc.vector.tensor_tensor(wts[:, c % 2, :], acts[:, c % 2, :], gates[:, tile % TILES, head, :],
                                             ALU.mult), wts_ready, "wts")

            def slot_u(c, s):
                tile, n = c // PH, c * SLOTS + s
                dve.wait_ge(u_landed[n % U_RING], 16 * (n // U_RING + 1))
                row = u_ring[:, n % U_RING, :]
                tell(nc.vector.scalar_tensor_tensor(
                    out=row, in0=row, scalar=1.0, in1=h2[:, tile % TILES, :],
                    op0=ALU.mult, op1=ALU.mult, accum_out=dots[:, c % 2, s:s + 1]), u_used, "u_used")

            def slot_v(c, s):
                if not by_vector(s):
                    return
                tile, n = c // PH, c * SLOTS + s
                dve.wait_ge(v_landed[n % V_RING], 16 * (n // V_RING + 1))
                v = xs[:, tile % TILES, :]
                tell(nc.vector.scalar_tensor_tensor(out=v, in0=v_ring[:, n % V_RING, :],
                                                    scalar=wts[:, c % 2, s:s + 1], in1=v,
                                                    op0=ALU.mult, op1=ALU.add), v_added, "v_added")

            interleave(front, slot_u, slot_v, begin)
            add_tile(LAYERS * TILES - 1)

        @block.tensor
        def _(pe):
            count = Count()
            weights = [0]

            def fill_act():
                n = count.next("act")
                if n > ACT_BANKS:
                    pe.wait_ge(act_emptied, n - ACT_BANKS)
                return act_bank[(n - 1) % ACT_BANKS]

            def fill_dve():
                n = count.next("dve")
                if n > DVE_BANKS:
                    pe.wait_ge(dve_emptied, n - DVE_BANKS)
                return dve_bank[(n - 1) % DVE_BANKS]

            def all_emptied():
                pe.wait_ge(act_emptied, count.n["act"])

            def flip(blocks):
                b = fill_act()
                for j, block_ in enumerate(blocks):
                    ins = nc.tensor.transpose(b[:, j * P:(j + 1) * P], block_, ident[:])
                ins.then_inc(act_filled, 1)

            def next_weights():
                n = weights[0]
                weights[0] += 1
                pe.wait_ge(w_loaded[n % W_RING], 16 * (n // W_RING + 1))
                return w_ring[:, n % W_RING]

            def flip_tile(source):
                for g in range(2):
                    flip([source[:, (4 * g + j) * P:(4 * g + j + 1) * P] for j in range(4)])

            def product(b, i, w, half):
                for c in range(half * KC // 2, (half + 1) * KC // 2):
                    ins = nc.tensor.matmul(b[:], hT[:, c, i * P:(i + 1) * P], w[:, c, :],
                                           start=(c == 0), stop=(c == KC - 1))
                return ins

            pe.wait_ge(consts_ready, 1)

            def front(k):
                l, t0 = k // HALVES, (k % HALVES) * HALF
                for p in range(NORM_PARTS):
                    if 2 <= p < 2 + HALF:
                        pe.wait_ge(h1_ready, k * HALF + p - 1)
                        flip_tile(h1[:, p - 2, :])
                    yield
                all_emptied()
                w_of_out = []
                for p in range(MID_STEPS):
                    if product_at(p):
                        kind, j, i = product_at(p)
                        if kind == "query":
                            pe.wait_ge(act_emptied, emptied(k, "h2T", 2))
                            w = next_weights()
                            b = fill_act()
                            query(b, w, 0, 0)
                            yield
                            query(b, w, 0, 1).then_inc(act_filled, 1)
                            yield
                        else:
                            if kind == "in":
                                if i == 0:
                                    w = next_weights()
                                b, filled = fill_act(), act_filled
                            else:
                                if i == 0:
                                    w_of_out.append(next_weights())
                                w = w_of_out[j]
                                if j == 0:
                                    pe.wait_ge(act_emptied, emptied(k, "mixT", 2 * (i + 1)))
                                b, filled = fill_dve(), dve_filled
                            product(b, i, w, 0)
                            yield
                            product(b, i, w, 1).then_inc(filled, 1)
                            yield
                    if p == LR_AT:
                        pe.wait_ge(small_loaded, SMALL_LOADS)
                        b_lr = fill_act()
                        for c in range(KC):
                            ins = nc.tensor.matmul(b_lr[0:RANK, 0:HTOK], w_lr[:, l, c, :], hT[:, c, :],
                                                   start=(c == 0), stop=(c == KC - 1))
                        ins.then_inc(act_filled, 1)
                    i = p - QK_FLIP_AT
                    if 0 <= i < HALF:
                        pe.wait_ge(qk_ready, k * HALF + i + 1)
                        for j in range(2):
                            flip([dqk[:, i, j * QH + h * P:j * QH + (h + 1) * P] for h in range(HEADS)])
                    attend(k, t0, p - ATTN_AT)
                    for i in range(HALF):
                        linear(k, l, t0, i, p - GLA_AT[i])
                    for i in range(HALF):
                        if p == MIX_AT[i]:
                            pe.wait_ge(mix_ready, k * HALF + i + 1)
                            flip_tile(mix[:, i, :])
                        if p == QUERY_AT + 2 and i == 0:
                            pe.wait_ge(keys_loaded, 16 * (l + 1))
                            pe.wait_ge(act_emptied, emptied(k, "route", 1))
                            score(0, 0)
                        if p == STATS_AT[i] + 2:
                            pe.wait_ge(h2_ready, k * HALF + i + 1)
                            flip_tile(h2[:, t0 + i, :])
                    yield
                for p in range(ROUTE_PARTS):
                    if p == 0:
                        pe.wait_ge(act_emptied, emptied(k, "h2T", 2 * HALF))
                        b = fill_act()
                        query(b, w, 1, 0)
                    if p == 1:
                        query(b, w, 1, 1).then_inc(act_filled, 1)
                    if p == 3:
                        pe.wait_ge(act_emptied, emptied(k, "route", 3))
                        score(0, 1)
                    j, part = divmod(p + ROUTE_LEAD, ROUTE_STEP)
                    if 0 < j < QJ and part < GPC:
                        if part == 0:
                            w = next_weights()
                        g, s = divmod(part, 2)
                        if s == 0:
                            b = fill_act()
                        for c in range(KC):
                            ins = nc.tensor.matmul(b[:, s * HTOK:(s + 1) * HTOK], w[:, c, part * P:(part + 1) * P],
                                                   hT[:, c, :], start=(c == 0), stop=(c == KC - 1))
                        if s == 1:
                            ins.then_inc(act_filled, 1)
                    if 0 < j < QJ and part == GPC + 1:
                        pe.wait_ge(act_emptied, emptied(k, "route", queried(j)))
                        for i in range(HALF):
                            score(j, i)
                    yield

            def query(b, w, i, half):
                for g in range(half * GPC // 2, (half + 1) * GPC // 2):
                    for c in range(KC):
                        ins = nc.tensor.matmul(b[:, g * P:(g + 1) * P], w[:, c, g * P:(g + 1) * P],
                                               hT[:, c, i * P:(i + 1) * P], start=(c == 0), stop=(c == KC - 1))
                return ins

            def score(j, i):
                b = fill_act()
                for g in range(GPC):
                    ins = nc.tensor.matmul(b[:, g * P:(g + 1) * P], qpT[:, j % 2, g, i * P:(i + 1) * P],
                                           keysT[:, GPC * j + g, :], start=True, stop=True)
                ins.then_inc(act_filled, 1)

            def attend(k, t0, at):
                step, part = divmod(at, ATTN_STEP)
                last_i, last_hg = divmod(step - 1, HEADS // 2)
                last_tile = t0 + last_i
                after = 0 < step <= ATTN_STEPS
                if part == 0 and after:
                    pe.wait_ge(a_ready, k * ATTN_STEPS + step)
                    for h in range(2):
                        flip([probs[:, 2 * h, j * P:(j + 1) * P] for j in range(last_tile + 1)])
                if at == 0:
                    pe.wait_ge(act_emptied, emptied(k, "qkT", 2 * HALF))
                if part < 2 and 0 <= step < ATTN_STEPS:
                    i, hg = divmod(step, HEADS // 2)
                    keys = (t0 + i + 1) * P
                    h = 2 * hg + part
                    for m in range(2):
                        rows = slice(m * DD, (m + 1) * DD)
                        b = fill_dve()
                        nc.tensor.matmul(b[:, 0:keys], qT[rows, h, i * P:(i + 1) * P], kT[rows, h, 0:keys],
                                         start=True, stop=True).then_inc(dve_filled, 1)
                if part == 2 and after:
                    pe.wait_ge(act_emptied, emptied(k, "aT", 2 * step))
                    b = fill_dve()
                    for h in range(2):
                        head = 2 * last_hg + h
                        for j in range(last_tile + 1):
                            ins = nc.tensor.matmul(b[:, h * HD:(h + 1) * HD], aT[:, head, j * P:(j + 1) * P],
                                                   v_nat[:, j, head * HD:(head + 1) * HD],
                                                   start=(j == 0), stop=(j == last_tile))
                    ins.then_inc(dve_filled, 1)

            def linear(k, l, t0, i, part):
                T = k * HALF + i
                qd, ki, kdc, _, qkiT = gla_scratch(t0)
                g_log = gates_of[i][1]
                if part == 0:
                    pe.wait_ge(act_emptied, emptied(k, "lr", 1))
                    b = fill_dve()
                    nc.tensor.matmul(b[:, 0:GK], lrT[:, i * P:(i + 1) * P], w_gate[:, l, :],
                                     start=True, stop=True).then_inc(dve_filled, 1)
                if part == 4:
                    pe.wait_ge(g_ready, T + 1)
                    b = fill_act()
                    nc.tensor.matmul(b[:, 0:GK], tri[:], g_log, start=True, stop=True)
                    nc.tensor.matmul(b[:, GK:2 * GK], suffix[:], g_log, start=True, stop=True).then_inc(act_filled, 1)
                    b = fill_act()
                    for pair in range(PAIRS):
                        ins = nc.tensor.matmul(b[:, 2 * pair:2 * pair + 2], g_log[:, pair * P:(pair + 1) * P], in_chunk[:],
                                               start=True, stop=True)
                    ins.then_inc(act_filled, 1)
                if part == 7:
                    pe.wait_ge(gla_ready, T + 1)
                    flip([qd[:, 0:P], qd[:, P:2 * P], ki[:, 0:P], ki[:, P:2 * P]])
                if part == 9:
                    pe.wait_ge(act_emptied, emptied(k, "gla", 3 * (i + 1)))
                    for s in range(2):
                        rows = slice(s * GD, (s + 1) * GD)
                        b = fill_dve()
                        for pair in range(PAIRS):
                            ins = nc.tensor.matmul(b[:, pair * P:(pair + 1) * P], qkiT[rows, 2 + pair, :],
                                                   qkiT[rows, pair, :], start=True, stop=True)
                        ins.then_inc(dve_filled, 1)
                if part in (10, 12):
                    c = (part - 10) // 2
                    b = fill_dve()
                    for pair in range(PAIRS):
                        cols = slice(pair * 2 * HD, (pair + 1) * 2 * HD)
                        ins = nc.tensor.matmul(b[:, cols], kdc[:, c, pair * P:(pair + 1) * P],
                                               gla_in[:, i, W_COLS + cols.start:W_COLS + cols.stop],
                                               start=True, stop=True)
                    ins.then_inc(dve_filled, 1)
                if part == 12:
                    pe.wait_ge(dve_emptied, read(k, "gla", 6 * i + 4))
                    b = fill_dve()
                    for h in range(HEADS):
                        nc.tensor.matmul(b[:, h * HD:(h + 1) * HD], a_intra[:, h, :],
                                         gla_in[:, i, W_COLS + h * HD:W_COLS + (h + 1) * HD],
                                         start=(h == 0), stop=False, skip_group_check=True)
                    for c in range(2):
                        toks = slice(c * GLA_CHUNK, (c + 1) * GLA_CHUNK)
                        for pair in range(PAIRS):
                            ins = nc.tensor.matmul(b[toks, pair * 2 * HD:(pair + 1) * 2 * HD], qkiT[:, pair, toks],
                                                   state[:, c, pair, :], start=False,
                                                   stop=(c == 1 and pair == PAIRS - 1), skip_group_check=True)
                    ins.then_inc(dve_filled, 1)

            def slot_v(c, s):
                if by_vector(s):
                    return
                tile, head = divmod(c, PH)
                n = c * SLOTS + s
                e = head * TOPK + s
                last = head == PH - 1 and v_count(c, s) == (c + 1) * V_PE
                if e == 0 and tile > 0:
                    pe.wait_ge(peer_added, tile)
                pe.wait_ge(v_landed[n % V_RING], 16 * (n // V_RING + 1))
                pe.wait_ge(diag_ready, v_count(c, s))
                for j in range(D // 512):
                    ins = nc.tensor.matmul(peer_acc[:, j * 512:(j + 1) * 512], diag[:, (v_count(c, s) - 1) % DIAGS, :],
                                           v_ring[:, n % V_RING, j * 512:(j + 1) * 512],
                                           start=(e == 0), stop=last)
                ins.then_inc(v_used, 1)

            interleave(front, lambda c, s: None, slot_v, lambda c: None)


_NAMES = ["x", "attn_norm_w", "w_in", "diff_q_norm_w", "diff_k_norm_w", "lambda_q1", "lambda_k1", "lambda_q2",
          "lambda_k2", "diff_out_norm_w", "gla_gate_w2", "gla_gate_b", "gla_out_norm_w", "w_out", "ffn_norm_w",
          "peer_w_q", "peer_sub_keys", "peer_u", "peer_v"]


def kernel(**inputs):
    import numpy as _np
    import concourse.bacc as _bacc
    from concourse import mybir as _mybir
    from concourse.bass_utils import run_bass_kernel_spmd as _run

    nc = _bacc.Bacc("TRN2", target_bir_lowering=False, num_devices=1, dynamic_dma_scratch_size=8192)
    arrays, args = {}, []
    for name in _NAMES:
        a = _np.asarray(inputs[name])
        if name == "peer_sub_keys":
            layers, heads, books, keys, width = a.shape
            a = a.transpose(0, 4, 1, 2, 3).reshape(layers, width, heads * books, keys)
        a = _np.ascontiguousarray(a)
        arrays[f"in_{name}"] = a
        args.append(nc.dram_tensor(f"in_{name}", a.shape, _mybir.dt.from_np(a.dtype), kind="ExternalInput").ap())
    shape = tuple(inputs["x"].shape)
    args.append(nc.dram_tensor("out_0", shape, _mybir.dt.float32, kind="ExternalOutput").ap())
    trunk(nc, *args)
    r = _run(nc, [arrays], core_ids=[0])
    return r.results[0]["out_0"]
```
